# Optimizing a Trainium2 kernel written in Bass

```python
import jax, jax.numpy as jnp
from jax import lax
import numpy as np

D_MODEL = 1024
BATCH = 1
SEQ = 256
DEPTH = 2

HEAD_DIM = 64
CONV_CH = D_MODEL // 4
FOX_HEADS = (D_MODEL // 4) // HEAD_DIM
DIL_HEADS = (D_MODEL // 2) // HEAD_DIM
FOX_W = FOX_HEADS * HEAD_DIM
DIL_W = DIL_HEADS * HEAD_DIM
CONV_K = 31
DIL_CONFIGS = ((128, 1), (512, 4), (2048, 16))
BLK = 128
ROPE_THETA = 10000.0
D_FF = 2816
ALPHA = (2 * DEPTH) ** 0.25
BETA = (8 * DEPTH) ** -0.25
LN_EPS = 1e-5
FORGET_BIAS_CENTER = 3.0
IN_WIDTHS = (CONV_CH, CONV_CH, FOX_W, FOX_W, FOX_W, FOX_HEADS, DIL_W, DIL_W, DIL_W)
IN_COLS = sum(IN_WIDTHS)
SPLIT_POINTS = tuple(int(v) for v in np.cumsum(IN_WIDTHS)[:-1])

kernel_name = "hymba_style_conv_fox_dilated_deepnorm"

def layer_norm(x, g, b):
    xf = x.astype(jnp.float32)
    mu = jnp.mean(xf, axis=-1, keepdims=True)
    var = jnp.mean(jnp.square(xf - mu), axis=-1, keepdims=True)
    return ((xf - mu) * lax.rsqrt(var + LN_EPS)).astype(x.dtype) * g + b

def swiglu_ffn(x, w_in, w_out):
    gate, up = jnp.split(x @ w_in, 2, axis=-1)
    return (jax.nn.silu(gate) * up) @ w_out

def rope(t, positions):
    inv = 1.0 / (ROPE_THETA ** (jnp.arange(0, HEAD_DIM, 2, dtype=jnp.float32) / HEAD_DIM))
    ang = positions.astype(jnp.float32)[:, None] * inv[None, :]
    ang = jnp.concatenate([ang, ang], axis=-1)
    cos = jnp.cos(ang).astype(t.dtype)
    sin = jnp.sin(ang).astype(t.dtype)
    t1, t2 = jnp.split(t, 2, axis=-1)
    return t * cos + jnp.concatenate([-t2, t1], axis=-1) * sin

def conv_module(val, gate, conv_w, conv_b, g, b):
    u = val * jax.nn.sigmoid(gate)
    u = lax.conv_general_dilated(
        u, conv_w[:, None, :].astype(u.dtype), window_strides=(1,),
        padding=[(CONV_K - 1, 0)], dimension_numbers=('NWC', 'WIO', 'NWC'),
        feature_group_count=CONV_CH) + conv_b
    return jax.nn.silu(layer_norm(u, g, b))

def forgetting_attention(q, k, v, f_logit, f_bias):
    bsz, nh, s_len, dh = q.shape
    log_f = jax.nn.log_sigmoid((f_logit + f_bias).astype(jnp.float32))
    cum = jnp.cumsum(log_f, axis=1).transpose(0, 2, 1)
    nq = s_len // BLK
    qb = q.reshape(bsz, nh, nq, BLK, dh).transpose(2, 0, 1, 3, 4)
    cb = cum.reshape(bsz, nh, nq, BLK).transpose(2, 0, 1, 3)
    kpos = jnp.arange(s_len)
    scale = HEAD_DIM ** -0.5

    def block(args):
        qi, ci, start = args
        s = jnp.einsum('bhqe,bhke->bhqk', qi, k).astype(jnp.float32) * scale
        s = s + (ci[..., :, None] - cum[..., None, :])
        qpos = start + jnp.arange(BLK)
        s = jnp.where(kpos[None, :] <= qpos[:, None], s, -jnp.inf)
        p = jax.nn.softmax(s, axis=-1)
        return jnp.einsum('bhqk,bhke->bhqe', p.astype(v.dtype), v)

    out = lax.map(block, (qb, cb, jnp.arange(nq) * BLK))
    return out.transpose(1, 2, 0, 3, 4).reshape(bsz, nh, s_len, dh)

def dilated_branch(q, k, v, window, dilation):
    bsz, nh, s_len, dh = q.shape
    span = window // dilation
    seg = dilation * BLK
    s_pad = -(-s_len // seg) * seg
    m_len = s_pad // dilation
    nb = m_len // BLK

    def to_sub(t):
        t = jnp.pad(t, ((0, 0), (0, 0), (0, s_pad - s_len), (0, 0)))
        t = t.reshape(bsz, nh, m_len, dilation, dh).transpose(0, 1, 3, 2, 4)
        return t.reshape(bsz, nh, dilation, nb, BLK, dh)

    def with_prev(t):
        prev = jnp.pad(t, ((0, 0), (0, 0), (0, 0), (1, 0), (0, 0), (0, 0)))[:, :, :, :-1]
        return jnp.concatenate([prev, t], axis=4)

    qs = to_sub(q)
    kw = with_prev(to_sub(k))
    vw = with_prev(to_sub(v))
    s = jnp.einsum('bhrnqe,bhrnke->bhrnqk', qs, kw).astype(jnp.float32)
    qm = jnp.arange(nb)[:, None, None] * BLK + jnp.arange(BLK)[None, :, None]
    km = jnp.arange(nb)[:, None, None] * BLK + jnp.arange(2 * BLK)[None, None, :] - BLK
    dist = qm - km
    valid = (km >= 0) & (dist >= 0) & (dist <= span)
    s = jnp.where(valid, s, -jnp.inf)
    mx = jnp.max(s, axis=-1, keepdims=True)
    p = jnp.exp(s - mx)
    den = jnp.sum(p, axis=-1, keepdims=True)
    o = jnp.einsum('bhrnqk,bhrnke->bhrnqe', (p / den).astype(v.dtype), vw)
    lse = (mx + jnp.log(den))[..., 0]
    o = o.reshape(bsz, nh, dilation, m_len, dh).transpose(0, 1, 3, 2, 4)
    o = o.reshape(bsz, nh, s_pad, dh)[:, :, :s_len]
    lse = lse.reshape(bsz, nh, dilation, m_len).transpose(0, 1, 3, 2)
    lse = lse.reshape(bsz, nh, s_pad)[:, :, :s_len]
    return o, lse

def dilated_attention(q, k, v):
    branches = [dilated_branch(q, k, v, w, d) for w, d in DIL_CONFIGS]
    outs = jnp.stack([o for o, _ in branches], axis=0)
    lses = jnp.stack([l for _, l in branches], axis=0)
    wts = jax.nn.softmax(lses, axis=0)
    return jnp.einsum('nbhs,nbhse->bhse', wts.astype(outs.dtype), outs)

def hybrid_mixer(x, w_in, w_o, f_bias, conv_w, conv_b, conv_g, conv_beta, positions):
    bsz, s_len, _ = x.shape
    proj = x @ w_in
    a_val, a_gate, bq, bk, bv, bf, cq, ck, cv = jnp.split(proj, SPLIT_POINTS, axis=-1)

    def heads(t, nh):
        return t.reshape(bsz, s_len, nh, HEAD_DIM).transpose(0, 2, 1, 3)

    def merge(t):
        return t.transpose(0, 2, 1, 3).reshape(bsz, s_len, -1)

    y_a = conv_module(a_val, a_gate, conv_w, conv_b, conv_g, conv_beta)
    y_b = forgetting_attention(heads(bq, FOX_HEADS), heads(bk, FOX_HEADS),
                               heads(bv, FOX_HEADS), bf, f_bias)
    qc = rope(heads(cq, DIL_HEADS), positions) * (HEAD_DIM ** -0.5)
    kc = rope(heads(ck, DIL_HEADS), positions)
    y_c = dilated_attention(qc, kc, heads(cv, DIL_HEADS))
    y = jnp.concatenate([y_a, merge(y_b), merge(y_c)], axis=-1)
    return y @ w_o

def setup_inputs(seed: int = 0) -> dict:
    key = jax.random.key(seed)
    ks = jax.random.split(key, 12)
    f32 = jnp.float32
    x = jax.random.normal(ks[0], (BATCH, SEQ, D_MODEL), f32)
    w_in = jax.random.normal(ks[1], (DEPTH, D_MODEL, IN_COLS), f32) * D_MODEL ** -0.5
    w_o = jax.random.normal(ks[2], (DEPTH, D_MODEL, D_MODEL), f32) * (D_MODEL ** -0.5) * BETA
    forget_bias = FORGET_BIAS_CENTER + 0.5 * jax.random.normal(ks[3], (DEPTH, FOX_HEADS), f32)
    conv_w = jax.random.normal(ks[4], (DEPTH, CONV_K, CONV_CH), f32) * CONV_K ** -0.5
    conv_b = 0.02 * jax.random.normal(ks[5], (DEPTH, CONV_CH), f32)
    conv_ln_g = 1.0 + 0.02 * jax.random.normal(ks[6], (DEPTH, CONV_CH), f32)
    conv_ln_b = 0.02 * jax.random.normal(ks[7], (DEPTH, CONV_CH), f32)
    ffn_w_in = jax.random.normal(ks[8], (DEPTH, 2, D_MODEL, 2 * D_FF), f32) * D_MODEL ** -0.5
    ffn_w_out = jax.random.normal(ks[9], (DEPTH, 2, D_FF, D_MODEL), f32) * (D_FF ** -0.5) * BETA
    ln_g = 1.0 + 0.02 * jax.random.normal(ks[10], (DEPTH, 3, D_MODEL), f32)
    ln_b = 0.02 * jax.random.normal(ks[11], (DEPTH, 3, D_MODEL), f32)
    return {"x": x, "w_in": w_in, "w_o": w_o, "forget_bias": forget_bias,
            "conv_w": conv_w, "conv_b": conv_b, "conv_ln_g": conv_ln_g,
            "conv_ln_b": conv_ln_b, "ffn_w_in": ffn_w_in, "ffn_w_out": ffn_w_out,
            "ln_g": ln_g, "ln_b": ln_b}

def reference(x, w_in, w_o, forget_bias, conv_w, conv_b, conv_ln_g, conv_ln_b,
              ffn_w_in, ffn_w_out, ln_g, ln_b):
    positions = jnp.arange(x.shape[1])
    h = x
    for l in range(DEPTH):
        h = layer_norm(ALPHA * h + 0.5 * swiglu_ffn(h, ffn_w_in[l, 0], ffn_w_out[l, 0]),
                       ln_g[l, 0], ln_b[l, 0])
        h = layer_norm(ALPHA * h + hybrid_mixer(h, w_in[l], w_o[l], forget_bias[l], conv_w[l],
                                                conv_b[l], conv_ln_g[l], conv_ln_b[l], positions),
                       ln_g[l, 1], ln_b[l, 1])
        h = layer_norm(ALPHA * h + 0.5 * swiglu_ffn(h, ffn_w_in[l, 1], ffn_w_out[l, 1]),
                       ln_g[l, 2], ln_b[l, 2])
    return h


_drawn_inputs = setup_inputs


def setup_inputs(seed=0):
    import zlib

    import numpy as np

    out = dict(_drawn_inputs(seed))
    spreads = {}
    factors = {'conv_b': 8.0, 'conv_ln_g': 22.221, 'conv_ln_b': 22.446, 'forget_bias': 26.488}
    for name, (base, spread) in spreads.items():
        noise = np.random.default_rng([zlib.crc32(name.encode()), seed]).standard_normal(out[name].shape)
        drawn = base * np.exp(spread * noise) if base else spread * noise
        out[name] = __import__('jax').numpy.asarray(drawn.astype(out[name].dtype))
    for name, factor in factors.items():
        out[name] = (out[name] * factor).astype(out[name].dtype)
    return out
```

```python
from contextlib import ExitStack

import numpy as np

import concourse.bass as bass
from concourse import mybir

F32 = mybir.dt.float32
F32R = mybir.dt.float32r
ALU = mybir.AluOpType
ACT = mybir.ActivationFunctionType
AX = mybir.AxisListType

P = 128
SEQ, D, DEPTH = 256, 1024, 2
T = SEQ // P
KT = D // P
BANK = 512
HALVES = D // BANK
HD = 64
CONV_CH, FOX_H, DIL_H, CONV_K = 256, 4, 8, 31
CB = CONV_CH // P
D_FF = 2816
CHUNK = 256
NCH = D_FF // CHUNK
ALPHA = (2 * DEPTH) ** 0.25
SCALE = (0.5, 1.0, 0.5)
EPS = 1e-5
MASKED = -(2.0 ** 100)

COL_CONV, COL_FQK, COL_FV = 0, 512, 1024
COL_CQ = COL_FV + FOX_H * HD + FOX_H
COL_CK, COL_CV = COL_CQ + DIL_H * HD, COL_CQ + 2 * DIL_H * HD
FVF = FOX_H * HD + FOX_H

FFN_UNITS = 3 * NCH
MIX_UNITS = 15
BASE = {0: 0, 1: FFN_UNITS, 2: FFN_UNITS + MIX_UNITS}
UNITS = 2 * FFN_UNITS + MIX_UNITS
RING = 3
UNIT = 4 * BANK
SLOT = KT * FVF
assert UNITS % RING == 0 and all(b % RING == 0 for b in BASE.values()) and SLOT >= UNIT

SLOTS = [("head", 0), ("head", 1), ("head", 2), ("head", 3), ("head", 4), ("head", 5), ("fq", 0), ("fk", 0),
         ("head", 6), ("head", 7), ("head", 8), ("conv", 0), ("head", 9), ("head", 10), ("convy", 0),
         ("head", 11)]
STEPS = len(SLOTS) + 2
HEADS = DIL_H + FOX_H
FILL = {0: (8, 0), 1: (8, 1), 2: (9, 0), 3: (9, 1), 4: (10, 0), 5: (10, 1), 6: (11, 0), 7: (11, 1),
        12: (12, 0), 13: (12, 1), 16: (13, 0), 17: (13, 1)}
SPLIT_AT = {2: 11, 4: 12, 6: 13, 8: 14, 14: 15}
WO_KT = {11: (4, 5), 12: (6, 7), 13: (0, 1), 14: (2, 3)}
Y_KT = (4, 5, 6, 7, 2, 3)
RSTD_AT, RSTD_CONV = (0, 4, 6), 2
CAUSAL = 3 * P
TAPS_AT = {}
_points = [4, 5, 6, 7] + [100 + s for s in range(10)]
for _n, _p in enumerate(_points):
    _a = 1 + _n * 4 if _n < 4 else 17 + (_n - 4) * 2
    TAPS_AT[_p] = range(min(_a, CONV_K), min(_a + (4 if _n < 4 else 2), CONV_K))
assert sum(len(r) for r in TAPS_AT.values()) == CONV_K - 1


def consts_array():
    pos = np.arange(SEQ, dtype=np.float32)
    inv = (1.0 / (np.float32(10000.0) ** (np.arange(0, HD, 2, dtype=np.float32) / np.float32(HD)))).astype(np.float32)
    ang = (pos[:, None] * inv[None, :]).astype(np.float32)
    cos = np.cos(ang).astype(np.float32).reshape(T, P, 32).transpose(1, 0, 2).reshape(P, -1)
    sin = np.sin(ang).astype(np.float32)
    sgn = np.concatenate([-sin, sin], axis=1).reshape(T, P, 64).transpose(1, 0, 2).reshape(P, -1)
    q, k = np.arange(SEQ)[:, None], np.arange(SEQ)[None, :]
    causal = k <= q
    count = (causal & (q - k <= 128)).astype(int) + (causal & ((q - k) % 4 == 0)) + (causal & ((q - k) % 16 == 0))
    dil = np.where(count > 0, np.log(np.maximum(count, 1)), MASKED).astype(np.float32)
    fox = np.where(causal, 0.0, MASKED).astype(np.float32)

    def tri(m):
        return np.concatenate([m[0:P, 0:P], m[P:, :]], axis=1)

    le = (np.arange(P)[:, None] <= np.arange(P)[None, :]).astype(np.float32)
    after = tri((q > k).astype(np.float32))
    eye = np.eye(P, dtype=np.float32)
    parts = [eye, eye * np.float32(ALPHA / SCALE[0]), eye * np.float32(ALPHA / SCALE[1]),
             np.ones((P, P), np.float32), le, after, tri(dil), tri(fox), cos, sgn]
    return np.concatenate([np.ascontiguousarray(p, np.float32) for p in parts], axis=1)


def trunk(nc, x, w_in, w_o, ffn_in, ffn_out, ln_gb, conv_wb, rows, consts, out):
    with ExitStack() as ctx:
        def sb(name, shape, dt=F32):
            return ctx.enter_context(nc.sbuf_tensor(name, shape, dt))

        def sem(name):
            return ctx.enter_context(nc.semaphore(name))

        raw = sb("raw", [P, RING, SLOT])
        w_hi = sb("w_hi", [P, RING, SLOT], F32R)
        w_lo = sb("w_lo", [P, RING, SLOT], F32R)
        xn = sb("xn", [P, T, D])
        xT_hi = sb("xT_hi", [P, KT, SEQ], F32R)
        xT_lo = sb("xT_lo", [P, KT, SEQ], F32R)
        yT_hi = sb("yT_hi", [P, KT, SEQ], F32R)
        yT_lo = sb("yT_lo", [P, KT, SEQ], F32R)
        hT_hi, hT_lo = yT_hi[:, 0:2, :], yT_lo[:, 0:2, :]
        gate = sb("gate", [P, T, CHUNK])
        hid = sb("hid", [P, T, CHUNK])
        gb = sb("gb", [P, 2, D])
        stats = sb("stats", [P, T, 2, 6])
        mv = sb("mv", [P, T, 2])
        vareps = sb("vareps", [P, T])
        rstd = sb("rstd", [P, T])
        cst = sb("cst", [P, consts.shape[1]])
        ident_r = sb("ident_r", [P, P], F32R)
        mask_hi = sb("mask_hi", [P, 2, CAUSAL], F32R)
        mask_lo = sb("mask_lo", [P, CAUSAL], F32R)
        small = sb("small", [P, rows.shape[2]])
        cwb = sb("cwb", [P, CB, CONV_K + 1])
        carrier = sb("carrier", [P, 2 * T])
        minus_half = sb("minus_half", [P, T])
        egate = sb("egate", [P, T, CONV_CH])
        conv_u = sb("conv_u", [P, T, CONV_CH])
        uT = sb("uT", [P, CB, CONV_K - 1 + SEQ])
        acc = sb("acc", [P, CB, SEQ])
        ya = sb("ya", [P, T, CONV_CH])
        yb = sb("yb", [P, T, CONV_CH])
        rope_c = sb("rope_c", [P, DIL_H * HD])
        rope_s = sb("rope_s", [P, DIL_H * HD])
        qk = sb("qk", [P, 2, DIL_H * HD])
        qT = sb("qT", [P, DIL_H // 2, SEQ])
        kT = sb("kT", [P, DIL_H // 2, SEQ])
        cv = sb("cv", [P, T, DIL_H * HD])
        fqk = sb("fqk", [P, T, 2 * FOX_H * HD])
        fqT = sb("fqT", [P, FOX_H // 2, SEQ])
        fkT = sb("fkT", [P, FOX_H // 2, SEQ])
        fv = sb("fv", [P, T, FOX_H * HD])
        fz = sb("fz", [P, T, FOX_H])
        fe = sb("fe", [P, T, FOX_H])
        fl = sb("fl", [P, T, FOX_H])
        lf = sb("lf", [P, T, FOX_H])
        lg = sb("lg", [P, FOX_H, CAUSAL])
        prob = sb("prob", [P, 2, CAUSAL])
        probT = sb("probT", [P, 2, CAUSAL])
        negmax = sb("negmax", [P, 2, T])
        den = sb("den", [P, 2, T])
        rden = sb("rden", [P, 2, T])
        bank = [ctx.enter_context(nc.psum_tensor(f"bank{i}", [P, BANK], F32)) for i in range(4)]
        ybank = [ctx.enter_context(nc.psum_tensor(f"ybank{i}", [P, BANK], F32)) for i in range(4)]

        at, view = 0, []
        for width in (P, P, P, P, P, CAUSAL, 2 * CAUSAL, T * 32, T * 64):
            view.append(cst[:, at:at + width])
            at += width
        ident, seed_ffn, seed_mix, ones, tri_le, tri_after, masks, cos_t, sin_t = view
        cos_t = cos_t.rearrange("p (t e) -> p t e", t=T)
        sin_t = sin_t.rearrange("p (t e) -> p t e", t=T)
        conv_g = small[:, 0:CONV_CH]
        conv_b = small[:, CONV_CH:2 * CONV_CH]
        fbias = small[:, 2 * CONV_CH:2 * CONV_CH + FOX_H]

        per = {}

        def counted(name, n):
            s = sem(name)
            per[name] = n
            return s

        raw_loaded = [counted(f"raw_loaded{i}", 32 * UNITS // RING) for i in range(RING)]
        hi_done = counted("hi_done", UNITS)
        lo_done = counted("lo_done", UNITS)
        unit_used = counted("unit_used", UNITS)
        gu_done = counted("gu_done", 2 * NCH * T)
        gate_ready = counted("gate_ready", 2 * NCH * T)
        h_ready = counted("h_ready", 2 * NCH * T)
        hT_psum = counted("hT_psum", 2 * NCH)
        hT_hi_done = counted("hT_hi_done", 2 * NCH)
        hT_ready = counted("hT_ready", 2 * NCH)
        y_done = counted("y_done", 3 * T)
        ln_step = counted("ln_step", 3 * T * 5)
        var_ready = counted("var_ready", 3 * T + T)
        rstd_ready = counted("rstd_ready", 3 * T + T)
        xn_ready = counted("xn_ready", 3 * T * HALVES)
        xT_psum = counted("xT_psum", 3 * T * HALVES)
        xT_hi_done = counted("xT_hi_done", 3 * T * HALVES)
        xT_ready = counted("xT_ready", 3 * T * HALVES)
        gb_loaded = counted("gb_loaded", 3 * 16)
        small_loaded = counted("small_loaded", 32)
        proj_done = counted("proj_done", 6 * T)
        egate_ready = counted("egate_ready", T)
        u_ready = counted("u_ready", T)
        rope_mul = counted("rope_mul", 2 * T)
        rope_ready = counted("rope_ready", 2 * T)
        cv_ready = counted("cv_ready", T)
        fqk_ready = counted("fqk_ready", T)
        fv_ready = counted("fv_ready", T)
        fz_ready = counted("fz_ready", T)
        lf_ready = counted("lf_ready", 1)
        fe_ready = counted("fe_ready", 1)
        fl_ready = counted("fl_ready", 2)
        lg_ready = counted("lg_ready", 1)
        uT_psum = counted("uT_psum", 1)
        uT_ready = counted("uT_ready", 1)
        qk_psum = counted("qk_psum", 2 * T + 2)
        qkT_ready = counted("qkT_ready", 2 * T + 2)
        conv_step = counted("conv_step", CB * CONV_K)
        convT_psum = counted("convT_psum", 1)
        cln_step = counted("cln_step", 3 * T)
        cln_ready = counted("cln_ready", T)
        ya_ready = counted("ya_ready", 1)
        yaT_psum = counted("yaT_psum", 1)
        yaT_hi_done = counted("yaT_hi_done", 1)
        yaT_ready = counted("yaT_ready", 1)
        s_done = counted("s_done", HEADS)
        mx_ready = counted("mx_ready", HEADS)
        exp_done = counted("exp_done", HEADS)
        rden_done = counted("rden_done", HEADS)
        p_ready = counted("p_ready", HEADS)
        pT_psum = counted("pT_psum", HEADS)
        pT_ready = counted("pT_ready", HEADS)
        pv_done = counted("pv_done", HEADS)
        y_hi_done = counted("y_hi_done", HEADS // 2)
        y_ready = counted("y_ready", HEADS // 2)
        x_loaded = sem("x_loaded")
        cst_loaded = sem("cst_loaded")
        setup_done = sem("setup_done")
        pool_setup = sem("pool_setup")
        uT_zero = sem("uT_zero")
        loads_begun = sem("loads_begun")
        stored = sem("stored")

        def count(s, l, k):
            return l * per[s.name] + k

        def unit_count(l, u):
            return l * UNITS + u + 1

        def slot_load(l, u_static, c=0):
            return (l * (UNITS // RING) + u_static // RING + c + 1) * 32

        block = ctx.enter_context(nc.Block())

        @block.sync
        def _(eng):
            w_in_v = w_in.rearrange("l (k p) n -> l p k n", p=P)
            ffn_in_v = ffn_in.rearrange("l w (k p) (g n) -> (l w) g p k n", p=P, g=2)
            ffn_out_v = ffn_out.rearrange("l w (k p) n -> (l w) p k n", p=P)
            w_o_v = w_o.rearrange("l (k p) n -> l p k n", p=P)
            ln_gb_v = ln_gb.rearrange("l j n -> (l j) n")

            def wait_apart(semaphore, value):
                eng.wait_ge(semaphore, value)
                eng.sem_inc(loads_begun, 1)

            def wait_slot(l, u):
                wait_apart(lo_done, unit_count(l, u))

            def load_ffn_in(l, w, u_static, u, half, c):
                wait_slot(l, u)
                s = u_static % RING
                for g in range(2):
                    dst = raw[:, s, 0:UNIT].rearrange("p (k g n) -> p k g n", k=4, g=2)[:, :, g, :]
                    src = ffn_in_v[bass.ds(2 * l + w, 1), g, :, 4 * half:4 * half + 4, bass.ds(c * CHUNK, CHUNK)]
                    eng.dma_start(dst, src.rearrange("a p k n -> (a p) k n")).then_inc(raw_loaded[s], 16)

            def load_ffn_out(l, w, u_static, u, c):
                wait_slot(l, u)
                s = u_static % RING
                for j in range(2):
                    dst = raw[:, s, 0:UNIT].rearrange("p (k n) -> p k n", k=2)[:, j, :]
                    src = ffn_out_v[bass.ds(2 * l + w, 1), :, bass.ds(2 * c + j, 1), :]
                    eng.dma_start(dst, src.rearrange("a p k n -> (a p) (k n)")).then_inc(raw_loaded[s], 16)

            def load_gb(l, j):
                wait_apart(xn_ready, count(xn_ready, l, 4 * j + 4))
                eng.dma_start(gb[:, :, :].rearrange("p a n -> p (a n)"),
                              ln_gb_v[bass.ds(3 * l + j, 1), :].broadcast_to([P, 2 * D])).then_inc(gb_loaded, 16)

            def ffn(l, w):
                b = BASE[2 * w]
                load_ffn_in(l, w, b, b, 0, 0)
                load_ffn_in(l, w, b + 1, b + 1, 1, 0)
                load_gb(l, 2 * w)
                with eng.Fori(1, NCH) as c:
                    load_ffn_in(l, w, b + 2, b + 3 * c - 1, 0, c)
                    load_ffn_in(l, w, b + 3, b + 3 * c, 1, c)
                    load_ffn_out(l, w, b + 4, b + 3 * c + 1, c - 1)
                load_ffn_out(l, w, b + FFN_UNITS - 1, b + FFN_UNITS - 1, NCH - 1)

            def load_unit(l, u, view, source):
                wait_slot(l, BASE[1] + u)
                k = source.shape[1] // 2
                for j in range(2):
                    eng.dma_start(view[:, j * k:j * k + k, :], source[:, j * k:j * k + k, :])\
                       .then_inc(raw_loaded[u % RING], 16)

            def mixer(l):
                w_l = w_in_v[bass.ds(l, 1)].rearrange("a p k n -> (a p) k n")
                o_l = w_o_v[bass.ds(l, 1)].rearrange("a p k n -> (a p) k n")
                for g, col in enumerate((COL_CONV, COL_CQ, COL_CK, COL_CV, COL_FQK)):
                    for half in range(2):
                        u = 2 * g + half
                        view = raw[:, u % RING, 0:UNIT].rearrange("p (k n) -> p k n", k=4)
                        load_unit(l, u, view, w_l[:, 4 * half:4 * half + 4, col:col + BANK])
                    if g == 0:
                        load_gb(l, 1)
                        eng.dma_start(small[:, :], rows[bass.ds(l, 1), 0, :].broadcast_to([P, rows.shape[2]]))\
                           .then_inc(small_loaded, 16)
                        eng.dma_start(cwb[:, :, :].rearrange("p c k -> p (c k)"),
                                      conv_wb[bass.ds(l, 1)].rearrange("a p n -> (a p) n")).then_inc(small_loaded, 16)
                view = raw[:, 10 % RING, :].rearrange("p (k n) -> p k n", k=KT)
                load_unit(l, 10, view, w_l[:, :, COL_FV:COL_FV + FVF])
                for u, (k0, _) in WO_KT.items():
                    view = raw[:, u % RING, 0:UNIT].rearrange("p (k n) -> p k n", k=2)
                    load_unit(l, u, view, o_l[:, k0:k0 + 2, :])

            eng.dma_start(cst[:, :], consts).then_inc(cst_loaded, 16)
            for t in range(T):
                eng.dma_start(xn[:, t, :], x[t * P:(t + 1) * P, :]).then_inc(x_loaded, 16)
            with eng.Fori(0, DEPTH) as l:
                ffn(l, 0)
                mixer(l)
                ffn(l, 1)
            for t in range(T):
                eng.wait_ge(xn_ready, count(xn_ready, DEPTH, HALVES * (t + 1)))
                eng.dma_start(out[t * P:(t + 1) * P, :], xn[:, t, :]).then_inc(stored, 16)
            eng.wait_ge(stored, 16 * T)

        @block.tensor
        def _(eng):
            def wait_unit(l, u):
                eng.wait_ge(lo_done, unit_count(l, u) + RING)

            def frees(first, signal):
                if signal is not None:
                    first.then_inc(signal, 1)

            def transposes(dst, blocks, last_unit=None):
                for n, blk in enumerate(blocks):
                    m = eng.transpose(dst[:, n * P:(n + 1) * P], blk, ident)
                    if n == 0:
                        frees(m, last_unit)
                return m

            def stage_x(l, j, t):
                for h in range(HALVES):
                    if t > 0:
                        eng.wait_ge(xT_ready, count(xT_ready, l, 4 * j + h + 1))
                    eng.wait_ge(xn_ready, count(xn_ready, l, 4 * j + 2 * t + h + 1))
                    blocks = [xn[:, t, (4 * h + k) * P:(4 * h + k + 1) * P] for k in range(4)]
                    transposes(bank[2 + h], blocks, unit_used if t == h == 0 else None).then_inc(xT_psum, 1)

            def seed(t, scaled_ident):
                for h in range(HALVES):
                    m = eng.matmul(ybank[2 * t + h][:, :], scaled_ident, xn[:, t, h * BANK:(h + 1) * BANK],
                                   start=True, stop=False)
                    if h == 0:
                        first = m
                return first

            def project(dst, slot, half, t, width=BANK, kts=4, last_unit=None):
                wh = w_hi[:, slot, 0:kts * width].rearrange("p (k n) -> p k n", k=kts)
                wl = w_lo[:, slot, 0:kts * width].rearrange("p (k n) -> p k n", k=kts)
                tok = slice(t * P, (t + 1) * P)
                for k in range(kts):
                    kk = kts * half + k
                    m = eng.matmul(dst, xT_hi[:, kk, tok], wh[:, k, :], start=kk == 0, stop=False)
                    if k == 0:
                        frees(m, last_unit)
                    eng.matmul(dst, xT_hi[:, kk, tok], wl[:, k, :], start=False, stop=False)
                    m = eng.matmul(dst, xT_lo[:, kk, tok], wh[:, k, :], start=False, stop=kk == KT - 1)
                return m

            def out_product(slot, aT_hi, aT_lo, t, last, last_unit=None):
                wh = w_hi[:, slot, 0:UNIT].rearrange("p (k n) -> p k n", k=2)
                wl = w_lo[:, slot, 0:UNIT].rearrange("p (k n) -> p k n", k=2)
                tok = slice(t * P, (t + 1) * P)
                for h in range(HALVES):
                    dst, cols = ybank[2 * t + h][:, :], slice(h * BANK, (h + 1) * BANK)
                    for k in range(2):
                        m = eng.matmul(dst, aT_hi[:, k, tok], wh[:, k, cols], start=False, stop=False)
                        if h == k == 0:
                            frees(m, last_unit)
                        eng.matmul(dst, aT_hi[:, k, tok], wl[:, k, cols], start=False, stop=False)
                        m = eng.matmul(dst, aT_lo[:, k, tok], wh[:, k, cols], start=False, stop=last and k == 1)
                return m

            def hidden_T(last_unit=None):
                transposes(bank[2], [hid[:, t, j * P:(j + 1) * P] for j in range(2) for t in range(T)],
                           last_unit).then_inc(hT_psum, 1)

            def ffn(l, w):
                b, f = BASE[2 * w], w * NCH
                s = [(b + n) % RING for n in range(RING)]
                for t in range(T):
                    stage_x(l, 2 * w, t)
                    seed(t, seed_ffn)
                    eng.wait_ge(xT_ready, count(xT_ready, l, 8 * w + 2 * t + 2))
                    wait_unit(l, b)
                    m = project(bank[t][:, :], s[0], 0, t)
                    if t == T - 1:
                        m.then_inc(unit_used, 1)
                    wait_unit(l, b + 1)
                    project(bank[t][:, :], s[1], 1, t).then_inc(gu_done, 1)
                eng.wait_ge(h_ready, count(h_ready, l, f * T + T))
                hidden_T(unit_used)
                with eng.Fori(1, NCH) as c:
                    wait_unit(l, b + 3 * c - 1)
                    project(bank[0][:, :], s[2], 0, 0)
                    project(bank[1][:, :], s[2], 0, 1).then_inc(unit_used, 1)
                    wait_unit(l, b + 3 * c)
                    for t in range(T):
                        project(bank[t][:, :], s[0], 1, t).then_inc(gu_done, 1)
                    wait_unit(l, b + 3 * c + 1)
                    eng.wait_ge(hT_ready, count(hT_ready, l, f + c))
                    out_product(s[1], hT_hi, hT_lo, 0, False, unit_used)
                    out_product(s[1], hT_hi, hT_lo, 1, False).then_inc(unit_used, 1)
                    eng.wait_ge(h_ready, count(h_ready, l, (f + 1) * T + c * T))
                    hidden_T()
                wait_unit(l, b + FFN_UNITS - 1)
                eng.wait_ge(hT_ready, count(hT_ready, l, f + NCH))
                for t in range(T):
                    out_product(s[2], hT_hi, hT_lo, t, True).then_inc(y_done, 1)

            def score_slot(l, s):
                kind, h = SLOTS[s]
                b = bank[s % 2]
                if s < 2:
                    eng.wait_ge(cv_ready, count(cv_ready, l, s + 1))
                else:
                    before, hb = SLOTS[s - 2]
                    if before == "head":
                        eng.wait_ge(exp_done, count(exp_done, l, hb + 1))
                    elif before in ("fq", "fk"):
                        eng.wait_ge(qkT_ready, count(qkT_ready, l, 5 + (before == "fk")))
                    elif before == "conv":
                        eng.wait_ge(cln_ready, count(cln_ready, l, T))
                    else:
                        eng.wait_ge(yaT_ready, count(yaT_ready, l, 1))
                if kind in ("fq", "fk"):
                    eng.wait_ge(fqk_ready, count(fqk_ready, l, T))
                    o = FOX_H * HD * (kind == "fk")
                    transposes(b, [fqk[:, t, o + p * P:o + (p + 1) * P] for p in range(2) for t in range(T)])\
                        .then_inc(qk_psum, 1)
                elif kind == "conv":
                    eng.wait_ge(conv_step, count(conv_step, l, CB * CONV_K))
                    transposes(b, [acc[:, cb, t * P:(t + 1) * P] for t in range(T) for cb in range(CB)])\
                        .then_inc(convT_psum, 1)
                elif kind == "convy":
                    eng.wait_ge(ya_ready, count(ya_ready, l, 1))
                    transposes(b, [yb[:, t, cb * P:(cb + 1) * P] for cb in range(CB) for t in range(T)])\
                        .then_inc(yaT_psum, 1)
                else:
                    fox = h >= DIL_H
                    n = h - DIL_H * fox
                    qs, ks = (fqT, fkT) if fox else (qT, kT)
                    r = slice((n % 2) * HD, (n % 2 + 1) * HD)
                    eng.wait_ge(qkT_ready, count(qkT_ready, l, 2 * T + 2 * fox))
                    eng.matmul(b[:, 0:CAUSAL], ident_r[:, :], mask_hi[:, int(fox), :], start=True, stop=False)
                    if fox:
                        eng.wait_ge(lg_ready, count(lg_ready, l, 1))
                        eng.matmul(b[:, 0:P], tri_le, lg[:, n, 0:P], start=False, stop=False)
                        eng.matmul(b[:, P:2 * P], ones, lg[:, n, 0:P], start=False, stop=False)
                        eng.matmul(b[:, P:CAUSAL], tri_le, lg[:, n, P:CAUSAL], start=False, stop=False)
                    else:
                        eng.matmul(b[:, 0:CAUSAL], ident_r[:, :], mask_lo[:, :], start=False, stop=False)
                    eng.matmul(b[:, 0:P], qs[r, n // 2, 0:P], ks[r, n // 2, 0:P], start=False, stop=False)
                    eng.matmul(b[:, P:CAUSAL], qs[r, n // 2, P:SEQ], ks[r, n // 2, :], start=False, stop=True)\
                       .then_inc(s_done, 1)

            def probs_T(l, h):
                eng.wait_ge(p_ready, count(p_ready, l, h + 1))
                if h > 0:
                    eng.wait_ge(pT_ready, count(pT_ready, l, h))
                transposes(bank[2], [prob[:, h % 2, i * P:(i + 1) * P] for i in range(3)]).then_inc(pT_psum, 1)

            def values(l, h):
                eng.wait_ge(pT_ready, count(pT_ready, l, h + 1))
                if h >= 2 and h % 2 == 0:
                    eng.wait_ge(y_ready, count(y_ready, l, h // 2))
                if h >= DIL_H:
                    eng.wait_ge(fv_ready, count(fv_ready, l, T))
                    v, n = fv, h - DIL_H
                else:
                    v, n = cv, h
                r = slice((h % 2) * HD, (h % 2 + 1) * HD)
                eng.matmul(bank[3][r, 0:SEQ], v[:, 0, n * HD:(n + 1) * HD], probT[:, h % 2, 0:SEQ],
                           start=True, stop=False)
                eng.matmul(bank[3][r, P:SEQ], v[:, 1, n * HD:(n + 1) * HD], probT[:, h % 2, SEQ:CAUSAL],
                           start=False, stop=True).then_inc(pv_done, 1)

            def fill(l, u, t):
                s = u % RING
                if t == 0:
                    wait_unit(l, BASE[1] + u)
                if u in (8, 9):
                    if u == 8 and t == 0:
                        eng.wait_ge(rope_mul, count(rope_mul, l, T))
                    m = project(ybank[t][:, :], s, u - 8, t)
                    if u == 9:
                        m.then_inc(proj_done, 1)
                    elif t == 1:
                        m.then_inc(unit_used, 1)
                elif u == 10:
                    if t == 0:
                        eng.wait_ge(rope_mul, count(rope_mul, l, 2 * T))
                    project(ybank[2 + t][:, 0:FVF], s, 0, t, FVF, KT, unit_used if t == 0 else None)\
                        .then_inc(proj_done, 1)
                else:
                    if t == 0:
                        if u == 13:
                            eng.wait_ge(yaT_ready, count(yaT_ready, l, 1))
                        else:
                            eng.wait_ge(y_ready, count(y_ready, l, {11: 2, 12: 4, 14: 6}[u]))
                    if u == 11 and t == 0:
                        eng.wait_ge(fqk_ready, count(fqk_ready, l, T))
                        eng.wait_ge(fv_ready, count(fv_ready, l, T))
                        eng.wait_ge(fz_ready, count(fz_ready, l, T))
                        frees(seed(0, seed_mix), unit_used)
                        seed(1, seed_mix)
                    k0 = WO_KT[u][0]
                    m = out_product(s, yT_hi[:, k0:k0 + 2, :], yT_lo[:, k0:k0 + 2, :], t, u == 14)
                    if u == 14:
                        m.then_inc(y_done, 1)
                    elif t == 1:
                        m.then_inc(unit_used, 1)

            def mixer(l):
                b = BASE[1]
                for t in range(T):
                    stage_x(l, 1, t)
                    eng.wait_ge(xT_ready, count(xT_ready, l, 4 + 2 * t + 2))
                    wait_unit(l, b)
                    m = project(bank[t][:, :], 0, 0, t)
                    if t == T - 1:
                        m.then_inc(unit_used, 1)
                    wait_unit(l, b + 1)
                    project(bank[t][:, :], 1, 1, t).then_inc(proj_done, 1)
                for g, dst in enumerate((ybank[0:2], ybank[2:4], bank[0:2]), 1):
                    if g == 3:
                        eng.wait_ge(u_ready, count(u_ready, l, T))
                    for half in range(2):
                        u = 2 * g + half
                        wait_unit(l, b + u)
                        for t in range(T):
                            m = project(dst[t][:, :], u % RING, half, t,
                                        last_unit=unit_used if g == 1 and half == t == 0 else None)
                            if half == 1:
                                m.then_inc(proj_done, 1)
                        if half == 0:
                            m.then_inc(unit_used, 1)
                    if g == 1:
                        eng.wait_ge(u_ready, count(u_ready, l, T))
                        transposes(bank[2], [conv_u[:, t, cb * P:(cb + 1) * P] for cb in range(CB) for t in range(T)],
                                   unit_used).then_inc(uT_psum, 1)
                    else:
                        for t in range(T):
                            n = 2 * (g - 2) + t
                            eng.wait_ge(rope_ready, count(rope_ready, l, n + 1))
                            if n == 1:
                                eng.wait_ge(uT_ready, count(uT_ready, l, 1))
                            if n >= 2:
                                eng.wait_ge(qkT_ready, count(qkT_ready, l, n - 1))
                            transposes(bank[3 - t], [qk[:, t, p * P:(p + 1) * P] for p in range(4)],
                                       unit_used if t == 0 else None).then_inc(qk_psum, 1)
                for s in range(STEPS):
                    if s < len(SLOTS):
                        score_slot(l, s)
                    if 0 <= s - 1 < len(SLOTS) and SLOTS[s - 1][0] == "head":
                        probs_T(l, SLOTS[s - 1][1])
                    if 0 <= s - 2 and SLOTS[s - 2][0] == "head":
                        values(l, SLOTS[s - 2][1])
                    if s in FILL:
                        fill(l, *FILL[s])
                for t in range(T):
                    fill(l, 14, t)

            eng.sem_inc(unit_used, RING - 1)
            eng.wait_ge(setup_done, 3)
            with eng.Fori(0, DEPTH) as l:
                ffn(l, 0)
                mixer(l)
                ffn(l, 1)

        @block.scalar
        def _(eng):
            def split_hi(l, b, u, c=0):
                s = (b + u) % RING
                width = SLOT if b == BASE[1] and u == 10 and isinstance(c, int) else UNIT
                eng.wait_ge(raw_loaded[s], slot_load(l, b + u, c))
                eng.wait_ge(unit_used, unit_count(l, b + u + 3 * c))
                eng.activation(w_hi[:, s, 0:width], raw[:, s, 0:width], ACT.Copy).then_inc(hi_done, 1)

            def stage_hi(l, j, tiles=range(T)):
                for t in tiles:
                    for h in range(HALVES):
                        eng.wait_ge(xT_psum, count(xT_psum, l, 4 * j + 2 * t + h + 1))
                        eng.activation(xT_hi[:, 4 * h:4 * h + 4, t * P:(t + 1) * P],
                                       bank[2 + h][:, :].rearrange("p (k n) -> p k n", k=4), ACT.Copy)\
                           .then_inc(xT_hi_done, 1)

            def silu(l, f, c, t):
                eng.wait_ge(gu_done, count(gu_done, l, f * T + t + 1 + c * T))
                eng.activation(gate[:, t, :], bank[t][:, 0:CHUNK], ACT.Silu).then_inc(gate_ready, 1)

            def hidden_hi(l, f, c):
                eng.wait_ge(hT_psum, count(hT_psum, l, f + 1 + c))
                eng.activation(hT_hi, bank[2][:, :].rearrange("p (k n) -> p k n", k=2), ACT.Copy)\
                   .then_inc(hT_hi_done, 1)

            def ffn(l, w):
                b, f = BASE[2 * w], w * NCH
                if w == 0:
                    stage_hi(l, 0, (0,))
                    split_hi(l, b, 0)
                    split_hi(l, b, 1)
                    stage_hi(l, 0, (1,))
                else:
                    stage_hi(l, 2)
                split_hi(l, b, 2)
                silu(l, f, 0, 0)
                split_hi(l, b, 3)
                silu(l, f, 0, 1)
                hidden_hi(l, f, 0)
                split_hi(l, b, 4)

                def chunk(c, ahead):
                    split_hi(l, b, 2, c)
                    silu(l, f, c, 0)
                    silu(l, f, c, 1)
                    if ahead:
                        split_hi(l, b, 3, c)
                    hidden_hi(l, f, c)
                    if ahead:
                        split_hi(l, b, 4, c)

                with eng.Fori(1, NCH - 1) as c:
                    chunk(c, True)
                chunk(NCH - 1, w == 0)

            def mixer(l):
                b = BASE[1]
                stage_hi(l, 1)
                split_hi(l, b, 2)
                for t in range(T):
                    eng.wait_ge(proj_done, count(proj_done, l, t + 1))
                    eng.activation(egate[:, t, :], bank[t][:, CONV_CH:2 * CONV_CH], ACT.Sigmoid)\
                       .then_inc(egate_ready, 1)
                    split_hi(l, b, 3 + t)
                split_hi(l, b, 5)
                eng.wait_ge(uT_psum, count(uT_psum, l, 1))
                eng.activation(uT[:, :, CONV_K - 1:], bank[2][:, :].rearrange("p (c n) -> p c n", c=CB), ACT.Copy)\
                   .then_inc(uT_ready, 1)
                split_hi(l, b, 6)
                split_hi(l, b, 7)
                for n in range(2 * T):
                    t = n % T
                    if n == T:
                        split_hi(l, b, 8)
                        split_hi(l, b, 9)
                        for tt in range(T):
                            eng.wait_ge(proj_done, count(proj_done, l, 3 * T + tt + 1))
                            eng.activation(cv[:, tt, :], bank[tt][:, :], ACT.Copy).then_inc(cv_ready, 1)
                    eng.wait_ge(qk_psum, count(qk_psum, l, n + 1))
                    dst = (qT, kT)[n // T]
                    eng.activation(dst[:, :, t * P:(t + 1) * P], bank[3 - t][:, :].rearrange("p (k n) -> p k n", k=4),
                                   ACT.Copy, scale=HD ** -0.5 if n < T else 1.0).then_inc(qkT_ready, 1)
                split_hi(l, b, 10)
                for s in range(STEPS):
                    if 0 <= s - 1 < len(SLOTS) and SLOTS[s - 1][0] == "head":
                        h = SLOTS[s - 1][1]
                        eng.wait_ge(pT_psum, count(pT_psum, l, h + 1))
                        eng.activation(probT[:, h % 2, :], bank[2][:, 0:CAUSAL], ACT.Copy).then_inc(pT_ready, 1)
                    kind, h = SLOTS[s] if s < len(SLOTS) else ("none", 0)
                    sc = bank[s % 2]
                    if kind == "head":
                        eng.wait_ge(mx_ready, count(mx_ready, l, h + 1))
                        for t, cols in enumerate((slice(0, P), slice(P, CAUSAL))):
                            e = eng.activation(prob[:, h % 2, cols], sc[:, cols], ACT.Exp,
                                               bias=negmax[:, h % 2, t:t + 1], accum_out=den[:, h % 2, t:t + 1])
                        e.then_inc(exp_done, 1)
                    elif kind in ("fq", "fk"):
                        n = 4 + (kind == "fk")
                        eng.wait_ge(qk_psum, count(qk_psum, l, n + 1))
                        dst = fqT if kind == "fq" else fkT
                        eng.activation(dst[:, :, :], sc[:, :].rearrange("p (k n) -> p k n", k=2), ACT.Copy,
                                       scale=HD ** -0.5 if kind == "fq" else 1.0).then_inc(qkT_ready, 1)
                    elif kind == "convy":
                        eng.wait_ge(yaT_psum, count(yaT_psum, l, 1))
                        eng.activation(yT_hi[:, 0:CB, :], sc[:, :].rearrange("p (k n) -> p k n", k=CB), ACT.Copy)\
                           .then_inc(yaT_hi_done, 1)
                    if s in (3, 4):
                        eng.wait_ge(proj_done, count(proj_done, l, 4 * T + s - 2))
                        eng.activation(fqk[:, s - 3, :], ybank[s - 3][:, :], ACT.Copy).then_inc(fqk_ready, 1)
                    if s in (5, 6):
                        eng.wait_ge(proj_done, count(proj_done, l, 5 * T + s - 4))
                        eng.activation(fv[:, s - 5, :], ybank[s - 3][:, 0:FOX_H * HD], ACT.Copy).then_inc(fv_ready, 1)
                    if s == 7:
                        eng.wait_ge(fe_ready, count(fe_ready, l, 1))
                        eng.activation(fl[:, :, :], fe[:, :, :], ACT.Exp).then_inc(fl_ready, 1)
                        eng.wait_ge(fl_ready, count(fl_ready, l, 1))
                        eng.activation(fl[:, :, :], fl[:, :, :], ACT.Ln, bias=1.0).then_inc(fl_ready, 1)
                    if s == 12:
                        eng.wait_ge(cln_ready, count(cln_ready, l, T))
                        eng.activation(yb[:, :, :], ya[:, :, :], ACT.Silu).then_inc(ya_ready, 1)
                    if s in SPLIT_AT:
                        split_hi(l, b, SPLIT_AT[s])
                    if s >= 2 and SLOTS[s - 2][0] == "head" and SLOTS[s - 2][1] % 2:
                        pair = SLOTS[s - 2][1] // 2
                        eng.wait_ge(pv_done, count(pv_done, l, 2 * pair + 2))
                        eng.activation(yT_hi[:, Y_KT[pair], :], bank[3][:, 0:SEQ], ACT.Copy).then_inc(y_hi_done, 1)
                split_hi(l, b, 16)

            with eng.Fori(0, DEPTH) as l:
                ffn(l, 0)
                mixer(l)
                ffn(l, 1)

        @block.vector
        def _(eng):
            def split_lo(l, b, u, c=0):
                s = (b + u) % RING
                width = SLOT if b == BASE[1] and u == 10 and isinstance(c, int) else UNIT
                eng.wait_ge(hi_done, count(hi_done, l, b + u + 1 + 3 * c))
                eng.tensor_tensor(w_lo[:, s, 0:width], raw[:, s, 0:width], w_hi[:, s, 0:width].bitcast(F32),
                                  ALU.subtract).then_inc(lo_done, 1)

            def stage_lo(l, j, t):
                for h in range(HALVES):
                    eng.wait_ge(xT_hi_done, count(xT_hi_done, l, 4 * j + 2 * t + h + 1))
                    part = (slice(None), slice(4 * h, 4 * h + 4), slice(t * P, (t + 1) * P))
                    eng.tensor_tensor(xT_lo[part], bank[2 + h][:, :].rearrange("p (k n) -> p k n", k=4),
                                      xT_hi[part].bitcast(F32), ALU.subtract).then_inc(xT_ready, 1)

            def wait_apart(semaphore, value, n):
                eng.wait_ge(semaphore, value)
                eng.memset(carrier[:, n:n + 1], 0.0)

            def layer_norm(l, j):
                def step(t, k):
                    return count(ln_step, l, 5 * (T * j + t) + k)

                for t in range(T):
                    eng.wait_ge(y_done, count(y_done, l, T * j + t + 1))
                    for h in range(HALVES):
                        eng.bn_stats(stats[:, t, h, :], ybank[2 * t + h][:, :]).then_inc(ln_step, 1)
                    wait_apart(ln_step, step(t, 2), t)
                    eng.bn_aggr(mv[:, t, :], stats[:, t, :, :].rearrange("p a b -> p (a b)")).then_inc(ln_step, 1)
                    eng.wait_ge(ln_step, step(t, 3))
                    eng.tensor_scalar(vareps[:, t:t + 1], mv[:, t, 1:2], EPS / SCALE[j] ** 2, None, ALU.add)\
                       .then_inc(var_ready, 1)
                    if t == 0:
                        eng.wait_ge(gb_loaded, count(gb_loaded, l, 16 * (j + 1)))
                    for h in range(HALVES):
                        cols = slice(h * BANK, (h + 1) * BANK)
                        eng.scalar_tensor_tensor(xn[:, t, cols], ybank[2 * t + h][:, :], mv[:, t, 0:1], gb[:, 0, cols],
                                                 ALU.subtract, ALU.mult).then_inc(ln_step, 1)
                    if t == 1 and j < 2:
                        stage_lo(l, j + 1, 0)
                    eng.wait_ge(rstd_ready, count(rstd_ready, l, RSTD_AT[j] + t + 1))
                    for h in range(HALVES):
                        cols = slice(h * BANK, (h + 1) * BANK)
                        eng.wait_ge(ln_step, step(t, 4 + h))
                        eng.scalar_tensor_tensor(xn[:, t, cols], xn[:, t, cols], rstd[:, t:t + 1], gb[:, 1, cols],
                                                 ALU.mult, ALU.add).then_inc(xn_ready, 1)
                if j < 2:
                    stage_lo(l, j + 1, 1)

            def gated(l, f, c, t):
                eng.wait_ge(gate_ready, count(gate_ready, l, f * T + t + 1 + c * T))
                eng.tensor_tensor(hid[:, t, :], gate[:, t, :], bank[t][:, CHUNK:2 * CHUNK], ALU.mult)\
                   .then_inc(h_ready, 1)

            def hidden_lo(l, f, c):
                eng.wait_ge(hT_hi_done, count(hT_hi_done, l, f + 1 + c))
                eng.tensor_tensor(hT_lo, bank[2][:, :].rearrange("p (k n) -> p k n", k=2), hT_hi.bitcast(F32),
                                  ALU.subtract).then_inc(hT_ready, 1)

            def ffn(l, w):
                b, f = BASE[2 * w], w * NCH
                if w == 0:
                    stage_lo(l, 0, 0)
                    split_lo(l, b, 0)
                    split_lo(l, b, 1)
                    stage_lo(l, 0, 1)
                split_lo(l, b, 2)
                gated(l, f, 0, 0)
                split_lo(l, b, 3)
                gated(l, f, 0, 1)
                hidden_lo(l, f, 0)
                split_lo(l, b, 4)

                def chunk(c, ahead):
                    split_lo(l, b, 2, c)
                    gated(l, f, c, 0)
                    gated(l, f, c, 1)
                    if ahead:
                        split_lo(l, b, 3, c)
                    hidden_lo(l, f, c)
                    if ahead:
                        split_lo(l, b, 4, c)

                with eng.Fori(1, NCH - 1) as c:
                    chunk(c, True)
                chunk(NCH - 1, w == 0)
                layer_norm(l, 2 * w)

            def gated_conv_input(l, t):
                eng.wait_ge(egate_ready, count(egate_ready, l, t + 1))
                eng.tensor_tensor(conv_u[:, t, :], bank[t][:, 0:CONV_CH], egate[:, t, :], ALU.mult)\
                   .then_inc(u_ready, 1)

            def rope(l, n):
                t, src = n % T, ybank[n]
                eng.wait_ge(proj_done, count(proj_done, l, T + n + 1))
                if n > 0:
                    eng.wait_ge(rope_ready, count(rope_ready, l, n))
                eng.tensor_tensor(rope_c[:, :].rearrange("p (g e) -> p g e", e=32),
                                  src[:, :].rearrange("p (g e) -> p g e", e=32),
                                  cos_t[:, t:t + 1, :].broadcast_to([P, 2 * DIL_H, 32]), ALU.mult)
                halves = dict(h=DIL_H, s=2)
                swapped = src[:, :].rearrange("p (h s e) -> p h s e", **halves)[:, :, ::-1, :]
                sin4 = sin_t[:, t, :].rearrange("p (h s e) -> p h s e", h=1, s=2).broadcast_to([P, DIL_H, 2, 32])
                eng.tensor_tensor(rope_s[:, :].rearrange("p (h s e) -> p h s e", **halves), swapped, sin4, ALU.mult)\
                   .then_inc(rope_mul, 1)

            def taps(l, which):
                for k in which:
                    for cb in range(CB):
                        src, w = uT[:, cb, k:k + SEQ], cwb[:, cb, k:k + 1]
                        if k == 0:
                            eng.tensor_scalar(acc[:, cb, :], src, w, cwb[:, cb, CONV_K:CONV_K + 1], ALU.mult, ALU.add)\
                               .then_inc(conv_step, 1)
                        else:
                            eng.wait_ge(conv_step, count(conv_step, l, CB * (k - 1) + cb + 1))
                            eng.scalar_tensor_tensor(acc[:, cb, :], src, w, acc[:, cb, :], ALU.mult, ALU.add)\
                               .then_inc(conv_step, 1)

            def conv_norm_first(l):
                src = bank[11 % 2]
                eng.wait_ge(convT_psum, count(convT_psum, l, 1))
                for t in range(T):
                    eng.bn_stats(stats[:, t, 0, :], src[:, t * CONV_CH:(t + 1) * CONV_CH]).then_inc(cln_step, 1)
                for t in range(T):
                    wait_apart(cln_step, count(cln_step, l, t + 1), T + t)
                    eng.bn_aggr(mv[:, t, :], stats[:, t, 0, :]).then_inc(cln_step, 1)
                for t in range(T):
                    eng.wait_ge(cln_step, count(cln_step, l, T + t + 1))
                    eng.tensor_scalar(vareps[:, t:t + 1], mv[:, t, 1:2], EPS, None, ALU.add).then_inc(var_ready, 1)
                    eng.scalar_tensor_tensor(ya[:, t, :], src[:, t * CONV_CH:(t + 1) * CONV_CH], mv[:, t, 0:1], conv_g,
                                             ALU.subtract, ALU.mult).then_inc(cln_step, 1)
                for t in range(T):
                    eng.wait_ge(rstd_ready, count(rstd_ready, l, RSTD_CONV + t + 1))
                    eng.wait_ge(cln_step, count(cln_step, l, 2 * T + t + 1))
                    eng.scalar_tensor_tensor(ya[:, t, :], ya[:, t, :], rstd[:, t:t + 1], conv_b, ALU.mult, ALU.add)\
                       .then_inc(cln_ready, 1)

            def log_gates(l):
                eng.wait_ge(fl_ready, count(fl_ready, l, 2))
                eng.scalar_tensor_tensor(lf[:, :, :], fz[:, :, :], 0.0, fl[:, :, :], ALU.min, ALU.subtract)\
                   .then_inc(lf_ready, 1)
                eng.wait_ge(lf_ready, count(lf_ready, l, 1))
                for h in range(FOX_H):
                    for t, cols in enumerate((slice(0, P), slice(P, CAUSAL))):
                        e = eng.tensor_scalar(lg[:, h, cols], tri_after[:, cols], lf[:, t, h:h + 1], None, ALU.mult)
                e.then_inc(lg_ready, 1)

            def row_max(l, s, h):
                eng.wait_ge(s_done, count(s_done, l, h + 1))
                for t, cols in enumerate((slice(0, P), slice(P, CAUSAL))):
                    e = eng.tensor_reduce(negmax[:, h % 2, t:t + 1], bank[s % 2][:, cols], AX.X, ALU.max, negate=True)
                e.then_inc(mx_ready, 1)

            def normalise(l, h):
                eng.wait_ge(exp_done, count(exp_done, l, h + 1))
                eng.reciprocal(rden[:, h % 2, :], den[:, h % 2, :]).then_inc(rden_done, 1)
                eng.wait_ge(rden_done, count(rden_done, l, h + 1))
                for t, cols in enumerate((slice(0, P), slice(P, CAUSAL))):
                    e = eng.tensor_scalar(prob[:, h % 2, cols], prob[:, h % 2, cols], rden[:, h % 2, t:t + 1], None,
                                          ALU.mult)
                e.then_inc(p_ready, 1)

            def y_split_lo(l, s):
                if s >= 2 and SLOTS[s - 2][0] == "head" and SLOTS[s - 2][1] % 2:
                    pair = SLOTS[s - 2][1] // 2
                    eng.wait_ge(y_hi_done, count(y_hi_done, l, pair + 1))
                    eng.tensor_tensor(yT_lo[:, Y_KT[pair], :], bank[3][:, 0:SEQ], yT_hi[:, Y_KT[pair], :].bitcast(F32),
                                      ALU.subtract).then_inc(y_ready, 1)

            def mixer(l):
                b = BASE[1]
                split_lo(l, b, 2)
                for t in range(T):
                    gated_conv_input(l, t)
                    split_lo(l, b, 3 + t)
                split_lo(l, b, 5)
                rope(l, 0)
                rope(l, 1)
                split_lo(l, b, 6)
                eng.wait_ge(small_loaded, count(small_loaded, l, 32))
                eng.wait_ge(uT_ready, count(uT_ready, l, 1))
                taps(l, range(1))
                taps(l, TAPS_AT[4])
                split_lo(l, b, 7)
                taps(l, TAPS_AT[5])
                split_lo(l, b, 8)
                rope(l, 2)
                rope(l, 3)
                taps(l, TAPS_AT[6])
                split_lo(l, b, 9)
                taps(l, TAPS_AT[7])
                split_lo(l, b, 10)
                for s in range(STEPS):
                    kind, h = SLOTS[s] if s < len(SLOTS) else ("none", 0)
                    if kind == "head":
                        row_max(l, s, h)
                    y_split_lo(l, s - 1)
                    if s in (5, 6):
                        eng.wait_ge(fv_ready, count(fv_ready, l, s - 4))
                        eng.tensor_tensor(fz[:, s - 5, :], ybank[s - 3][:, FOX_H * HD:FVF], fbias, ALU.add)\
                           .then_inc(fz_ready, 1)
                    if s == 6:
                        eng.wait_ge(fz_ready, count(fz_ready, l, T))
                        eng.scalar_tensor_tensor(fe[:, :, :], fz[:, :, :], -1.0, fz[:, :, :], ALU.mult, ALU.min)\
                           .then_inc(fe_ready, 1)
                    if s in SPLIT_AT:
                        split_lo(l, b, SPLIT_AT[s])
                    taps(l, TAPS_AT.get(100 + s, ()))
                    if s == 8:
                        log_gates(l)
                    if s == 11:
                        conv_norm_first(l)
                    if kind == "convy":
                        eng.wait_ge(yaT_hi_done, count(yaT_hi_done, l, 1))
                        eng.tensor_tensor(yT_lo[:, 0:CB, :], bank[s % 2][:, :].rearrange("p (k n) -> p k n", k=CB),
                                          yT_hi[:, 0:CB, :].bitcast(F32), ALU.subtract).then_inc(yaT_ready, 1)
                    if kind == "head":
                        normalise(l, h)
                y_split_lo(l, STEPS - 1)
                split_lo(l, b, 16)
                layer_norm(l, 1)

            eng.sem_inc(lo_done, RING)
            eng.memset(uT[:, :, 0:CONV_K - 1], 0.0)
            eng.wait_ge(cst_loaded, 16)
            eng.tensor_copy(ident_r[:, :], ident).then_inc(setup_done, 1)
            eng.tensor_copy(mask_hi[:, :, :], masks.rearrange("p (m n) -> p m n", m=2)).then_inc(setup_done, 1)
            eng.wait_ge(setup_done, 2)
            eng.tensor_tensor(mask_lo[:, :], masks[:, 0:CAUSAL], mask_hi[:, 0, :].bitcast(F32), ALU.subtract)\
               .then_inc(setup_done, 1)
            eng.wait_ge(x_loaded, 16 * T)
            eng.sem_inc(xn_ready, T * HALVES)
            with eng.Fori(0, DEPTH) as l:
                ffn(l, 0)
                mixer(l)
                ffn(l, 1)

        @block.gpsimd
        def _(eng):
            def deviations(l, base):
                for t in range(T):
                    eng.wait_ge(var_ready, count(var_ready, l, base + t + 1))
                    eng.tensor_tensor(rstd[:, t:t + 1], vareps[:, t:t + 1], minus_half[:, t:t + 1], ALU.pow)\
                       .then_inc(rstd_ready, 1)

            eng.memset(minus_half[:, :], -0.5).then_inc(pool_setup, 1)
            eng.wait_ge(pool_setup, 1)
            with eng.Fori(0, DEPTH) as l:
                deviations(l, RSTD_AT[0])
                for n in range(2 * T):
                    eng.wait_ge(rope_mul, count(rope_mul, l, n + 1))
                    if n >= T:
                        eng.wait_ge(qk_psum, count(qk_psum, l, n - T + 1))
                    eng.tensor_tensor(qk[:, n % T, :], rope_c[:, :], rope_s[:, :], ALU.add).then_inc(rope_ready, 1)
                deviations(l, RSTD_CONV)
                deviations(l, RSTD_AT[1])
                deviations(l, RSTD_AT[2])


def kernel(**inputs):
    import concourse.bacc as _bacc
    from concourse.bass_utils import run_bass_kernel_spmd as _run

    a = {k: np.ascontiguousarray(v) for k, v in inputs.items()}
    arrays = {
        "x": a["x"].reshape(SEQ, D), "w_in": a["w_in"], "w_o": a["w_o"],
        "ffn_in": a["ffn_w_in"], "ffn_out": a["ffn_w_out"],
        "ln_gb": np.concatenate([a["ln_g"], a["ln_b"]], axis=2),
        "conv_wb": np.ascontiguousarray(
            np.concatenate([a["conv_w"], a["conv_b"][:, None, :]], axis=1)
            .reshape(DEPTH, CONV_K + 1, CB, P).transpose(0, 3, 2, 1).reshape(DEPTH, P, CB * (CONV_K + 1))),
        "rows": np.concatenate([a["conv_ln_g"], a["conv_ln_b"], a["forget_bias"]], axis=1)[:, None, :],
        "consts": consts_array(),
    }
    arrays = {f"in_{k}": np.ascontiguousarray(v) for k, v in arrays.items()}
    nc = _bacc.Bacc("TRN2", target_bir_lowering=False, num_devices=1)
    args = [nc.dram_tensor(k, v.shape, mybir.dt.from_np(v.dtype), kind="ExternalInput").ap() for k, v in arrays.items()]
    out = nc.dram_tensor("out_dram", (SEQ, D), F32, kind="ExternalOutput").ap()
    trunk(nc, *args, out)
    r = _run(nc, [arrays], core_ids=[0])
    return r.results[0]["out_dram"].reshape(1, SEQ, D)
```

```python
from contextlib import ExitStack

import numpy as np

import concourse.bass as bass
from concourse import mybir

F32 = mybir.dt.float32
F32R = mybir.dt.float32r
ALU = mybir.AluOpType
ACT = mybir.ActivationFunctionType
AX = mybir.AxisListType

P = 128
SEQ, D, DEPTH = 256, 1024, 2
T = SEQ // P
KT = D // P
BANK = 512
HALVES = D // BANK
HD = 64
CONV_CH, FOX_H, DIL_H, CONV_K = 256, 4, 8, 31
CB = CONV_CH // P
D_FF = 2816
CHUNK = 256
NCH = D_FF // CHUNK
ALPHA = (2 * DEPTH) ** 0.25
SCALE = (0.5, 1.0, 0.5)
EPS = 1e-5
MASKED = -(2.0 ** 100)

COL_CONV, COL_FQK, COL_FV = 0, 512, 1024
COL_CQ = COL_FV + FOX_H * HD + FOX_H
COL_CK, COL_CV = COL_CQ + DIL_H * HD, COL_CQ + 2 * DIL_H * HD
FVF = FOX_H * HD + FOX_H

FFN_UNITS = 3 * NCH
MIX_UNITS = 15
BASE = {0: 0, 1: FFN_UNITS, 2: FFN_UNITS + MIX_UNITS}
UNITS = 2 * FFN_UNITS + MIX_UNITS
RING = 3
UNIT = 4 * BANK
SLOT = KT * FVF
assert UNITS % RING == 0 and all(b % RING == 0 for b in BASE.values()) and SLOT >= UNIT

SLOTS = [("head", 0), ("head", 1), ("head", 2), ("head", 3), ("head", 4), ("head", 5), ("fq", 0), ("fk", 0),
         ("head", 6), ("head", 7), ("conv", 0), ("head", 8), ("head", 9), ("convy", 0), ("head", 10),
         ("head", 11)]
CONV_SLOT = SLOTS.index(("conv", 0))
STEPS = len(SLOTS) + 2
HEADS = DIL_H + FOX_H
FILL = {0: [(8, 0, 0), (8, 0, 1)], 1: [(8, 1, 0)], 2: [(8, 1, 1), (9, 0, 0)], 3: [(9, 0, 1)],
        4: [(9, 1, 0), (9, 1, 1)], 5: [(10, 0, 0), (10, 0, 1)], 6: [(10, 1, 0)],
        7: [("open", 0, 0), (10, 1, 1)], 8: [(11, 0, 0)], 9: [("open", 1, 0), (11, 0, 1)], 10: [(11, 1, 0)],
        11: [(11, 1, 1)], 12: [(12, 0, 0)], 13: [(12, 0, 1)], 14: [(12, 1, 0), (12, 1, 1)],
        15: [(13, 0, 0)], 16: [(13, 0, 1)], 17: [(13, 1, 0)]}
TAIL = [(14, 0, 0), (14, 0, 1), (13, 1, 1), (14, 1, 0), (14, 1, 1)]
HI_AT = {1: 10, 3: 11, 6: 12, 10: 13, 12: 14, 15: 15}
FQK_AT = {4: 0, 5: 1}
FV_AT = {6: 0, 8: 1}
LF_STEP = 9
BEGIN_AT = {7: 0, 9: 1}
FREES_AT = {0: 7, 8: 10}
WO_KT = {11: (4, 5), 12: (6, 7), 13: (0, 1), 14: (2, 3)}
Y_KT = (4, 5, 6, 7, 2, 3)
RSTD_AT, RSTD_CONV = (0, 4, 6), 2
EARLY = P
CAUSAL = 3 * P
TAPS_AT = {}
_tap = 1
for _where, _n in [(("unit", 5), 5), (("unit", 6), 5), (("unit", 7), 4)] + \
        [(("step", s), n) for s, n in enumerate((1, 1, 2, 2, 2, 2, 2, 2, 1, 1))]:
    TAPS_AT[_where] = range(_tap, _tap + _n)
    _tap += _n
assert FILL[7][-1] == (10, 1, 1) and all(SLOTS[s][0] == "head" for s in FREES_AT)
assert sum(len(r) for r in TAPS_AT.values()) == CONV_K - 1


def consts_array():
    pos = np.arange(SEQ, dtype=np.float32)
    inv = (1.0 / (np.float32(10000.0) ** (np.arange(0, HD, 2, dtype=np.float32) / np.float32(HD)))).astype(np.float32)
    ang = (pos[:, None] * inv[None, :]).astype(np.float32)
    cos = np.cos(ang).astype(np.float32).reshape(T, P, 32).transpose(1, 0, 2).reshape(P, -1)
    sin = np.sin(ang).astype(np.float32)
    sgn = np.concatenate([-sin, sin], axis=1).reshape(T, P, 64).transpose(1, 0, 2).reshape(P, -1)
    q, k = np.arange(SEQ)[:, None], np.arange(SEQ)[None, :]
    causal = k <= q
    count = (causal & (q - k <= 128)).astype(int) + (causal & ((q - k) % 4 == 0)) + (causal & ((q - k) % 16 == 0))
    dil = np.where(count > 0, np.log(np.maximum(count, 1)), MASKED).astype(np.float32)
    fox = np.where(causal, 0.0, MASKED).astype(np.float32)

    def tri(m):
        return np.concatenate([m[0:P, 0:P], m[P:, :]], axis=1)

    le = (np.arange(P)[:, None] <= np.arange(P)[None, :]).astype(np.float32)
    after = tri((q > k).astype(np.float32))
    eye = np.eye(P, dtype=np.float32)
    parts = [eye, np.ones((P, P), np.float32), le, after, tri(dil), tri(fox), cos, sgn]
    return np.concatenate([np.ascontiguousarray(p, np.float32) for p in parts], axis=1)


def trunk(nc, x, w_in, w_o, ffn_in, ffn_out, ln_gb, conv_wb, rows, consts, out):
    with ExitStack() as ctx:
        def sb(name, shape, dt=F32):
            return ctx.enter_context(nc.sbuf_tensor(name, shape, dt))

        def sem(name):
            return ctx.enter_context(nc.semaphore(name))

        raw = sb("raw", [P, RING, SLOT])
        w_hi = sb("w_hi", [P, RING, SLOT], F32R)
        w_lo = sb("w_lo", [P, RING, SLOT], F32R)
        xn = sb("xn", [P, T, D])
        xT_hi = sb("xT_hi", [P, KT, SEQ], F32R)
        xT_lo = sb("xT_lo", [P, KT, SEQ], F32R)
        yT_hi = sb("yT_hi", [P, KT, SEQ], F32R)
        yT_lo = sb("yT_lo", [P, KT, SEQ], F32R)
        hT = [(yT_hi[:, k:k + 2, :], yT_lo[:, k:k + 2, :]) for k in (0, 2)]
        gate = sb("gate", [P, T, CHUNK])
        hid = sb("hid", [P, T, CHUNK])
        gb = sb("gb", [P, 2, D])
        stats = sb("stats", [P, T, 2, 6])
        mv = sb("mv", [P, T, 2])
        vareps = sb("vareps", [P, T])
        rstd = sb("rstd", [P, T])
        cst = sb("cst", [P, consts.shape[1]])
        ident_r = sb("ident_r", [P, P], F32R)
        mask_hi = sb("mask_hi", [P, 2, CAUSAL], F32R)
        mask_lo = sb("mask_lo", [P, CAUSAL], F32R)
        small = sb("small", [P, rows.shape[2]])
        cwb = sb("cwb", [P, CB, CONV_K + 1])
        warm = sb("warm", [P, T])
        carrier = sb("carrier", [P, 2 * T])
        minus_half = sb("minus_half", [P, T])
        egate = sb("egate", [P, T, CONV_CH])
        conv_u = sb("conv_u", [P, T, CONV_CH])
        uT = sb("uT", [P, CB, CONV_K - 1 + SEQ])
        acc = sb("acc", [P, CB, SEQ])
        ya = sb("ya", [P, T, CONV_CH])
        yb = sb("yb", [P, T, CONV_CH])
        rope_c = sb("rope_c", [P, DIL_H * HD])
        rope_s = sb("rope_s", [P, DIL_H * HD])
        qk = sb("qk", [P, 2, DIL_H * HD])
        qT = sb("qT", [P, DIL_H // 2, SEQ])
        kT = sb("kT", [P, DIL_H // 2, SEQ])
        cv = sb("cv", [P, T, DIL_H * HD])
        fqk = sb("fqk", [P, T, 2 * FOX_H * HD])
        fqT = sb("fqT", [P, FOX_H // 2, SEQ])
        fkT = sb("fkT", [P, FOX_H // 2, SEQ])
        fv = sb("fv", [P, T, FOX_H * HD])
        fz = sb("fz", [P, T, FOX_H])
        fe = sb("fe", [P, T, FOX_H])
        fl = sb("fl", [P, T, FOX_H])
        lf = sb("lf", [P, T, FOX_H])
        lg = sb("lg", [P, FOX_H, CAUSAL])
        prob = sb("prob", [P, 2, CAUSAL])
        probT = sb("probT", [P, 2, CAUSAL])
        negmax = sb("negmax", [P, 2, T])
        den = sb("den", [P, 2, T])
        rden = sb("rden", [P, 2, T])
        bank = [ctx.enter_context(nc.psum_tensor(f"bank{i}", [P, BANK], F32)) for i in range(4)]
        ybank = [ctx.enter_context(nc.psum_tensor(f"ybank{i}", [P, BANK], F32)) for i in range(4)]

        at, view = 0, []
        for width in (P, P, P, CAUSAL, 2 * CAUSAL, T * 32, T * 64):
            view.append(cst[:, at:at + width])
            at += width
        ident, ones, tri_le, tri_after, masks, cos_t, sin_t = view
        cos_t = cos_t.rearrange("p (t e) -> p t e", t=T)
        sin_t = sin_t.rearrange("p (t e) -> p t e", t=T)
        conv_g = small[:, 0:CONV_CH]
        conv_b = small[:, CONV_CH:2 * CONV_CH]
        fbias = small[:, 2 * CONV_CH:2 * CONV_CH + FOX_H]

        per = {}

        def counted(name, n):
            s = sem(name)
            per[name] = n
            return s

        raw_loaded = [counted(f"raw_loaded{i}", 32 * UNITS // RING) for i in range(RING)]
        hi_done = counted("hi_done", UNITS)
        lo_done = counted("lo_done", UNITS)
        unit_used = counted("unit_used", UNITS)
        gu_done = counted("gu_done", 2 * NCH * T)
        gate_ready = counted("gate_ready", 2 * NCH * T)
        h_ready = counted("h_ready", 2 * NCH * T)
        hT_psum = counted("hT_psum", 2 * NCH)
        hT_hi_done = counted("hT_hi_done", 2 * NCH)
        hT_ready = counted("hT_ready", 2 * NCH)
        sum_open = counted("sum_open", 3 * T * HALVES)
        sum_begun = counted("sum_begun", 3 * T * HALVES)
        y_done = counted("y_done", 3 * T * HALVES)
        ln_step = counted("ln_step", 3 * T * 5)
        var_ready = counted("var_ready", 3 * T + T)
        rstd_ready = counted("rstd_ready", 3 * T + T)
        xn_ready = counted("xn_ready", 3 * T * HALVES)
        xT_psum = counted("xT_psum", 3 * T * HALVES)
        xT_hi_done = counted("xT_hi_done", 3 * T * HALVES)
        xT_ready = counted("xT_ready", 3 * T * HALVES)
        gb_loaded = counted("gb_loaded", 3 * 16)
        small_loaded = counted("small_loaded", 32)
        proj_done = counted("proj_done", 6 * T)
        egate_ready = counted("egate_ready", T)
        u_ready = counted("u_ready", T)
        rope_mul = counted("rope_mul", 2 * T)
        rope_ready = counted("rope_ready", 2 * T)
        cv_ready = counted("cv_ready", T)
        fqk_ready = counted("fqk_ready", T)
        fv_ready = counted("fv_ready", T)
        fz_ready = counted("fz_ready", T)
        lf_ready = counted("lf_ready", 1)
        fe_ready = counted("fe_ready", 1)
        fl_ready = counted("fl_ready", 2)
        lg_ready = counted("lg_ready", 1)
        uT_psum = counted("uT_psum", 1)
        uT_ready = counted("uT_ready", 1)
        qk_psum = counted("qk_psum", 2 * T + 2)
        qkT_ready = counted("qkT_ready", 2 * T + 2)
        conv_step = counted("conv_step", CB * CONV_K)
        convT_psum = counted("convT_psum", 1)
        cln_step = counted("cln_step", 3 * T)
        cln_ready = counted("cln_ready", T)
        ya_ready = counted("ya_ready", 1)
        yaT_psum = counted("yaT_psum", 1)
        yaT_hi_done = counted("yaT_hi_done", 1)
        yaT_ready = counted("yaT_ready", 1)
        s_done = counted("s_done", HEADS)
        mx_ready = counted("mx_ready", HEADS)
        exp_done = counted("exp_done", HEADS)
        rden_done = counted("rden_done", HEADS)
        p_ready = counted("p_ready", HEADS)
        pT_psum = counted("pT_psum", HEADS)
        pT_ready = counted("pT_ready", HEADS)
        pv_done = counted("pv_done", HEADS)
        y_hi_done = counted("y_hi_done", HEADS // 2)
        y_ready = counted("y_ready", HEADS // 2)
        x0_loaded = sem("x0_loaded")
        x1_loaded = sem("x1_loaded")
        cst_loaded = sem("cst_loaded")
        tables_loaded = sem("tables_loaded")
        setup_done = sem("setup_done")
        pool_setup = sem("pool_setup")
        loads_begun = sem("loads_begun")
        stored = sem("stored")

        def count(s, l, k):
            return l * per[s.name] + k

        def unit_count(l, u):
            return l * UNITS + u + 1

        def slot_load(l, u_static, c=0):
            return (l * (UNITS // RING) + u_static // RING + c + 1) * 32

        block = ctx.enter_context(nc.Block())

        @block.sync
        def _(eng):
            w_in_v = w_in.rearrange("l (k p) n -> l p k n", p=P)
            ffn_in_v = ffn_in.rearrange("l w (k p) (g n) -> (l w) g p k n", p=P, g=2)
            ffn_out_v = ffn_out.rearrange("l w (k p) n -> (l w) p k n", p=P)
            w_o_v = w_o.rearrange("l (k p) n -> l p k n", p=P)
            ln_gb_v = ln_gb.rearrange("l j n -> (l j) n")

            def wait_apart(semaphore, value):
                eng.wait_ge(semaphore, value)
                eng.sem_inc(loads_begun, 1)

            def wait_slot(l, u):
                wait_apart(lo_done, unit_count(l, u))

            def load_ffn_in(l, w, u_static, u, half, c):
                wait_slot(l, u)
                s = u_static % RING
                for g in range(2):
                    dst = raw[:, s, 0:UNIT].rearrange("p (k g n) -> p k g n", k=4, g=2)[:, :, g, :]
                    src = ffn_in_v[bass.ds(2 * l + w, 1), g, :, 4 * half:4 * half + 4, bass.ds(c * CHUNK, CHUNK)]
                    eng.dma_start(dst, src.rearrange("a p k n -> (a p) k n")).then_inc(raw_loaded[s], 16)

            def load_ffn_out(l, w, u_static, u, c):
                wait_slot(l, u)
                s = u_static % RING
                for j in range(2):
                    dst = raw[:, s, 0:UNIT].rearrange("p (k n) -> p k n", k=2)[:, j, :]
                    src = ffn_out_v[bass.ds(2 * l + w, 1), :, bass.ds(2 * c + j, 1), :]
                    eng.dma_start(dst, src.rearrange("a p k n -> (a p) (k n)")).then_inc(raw_loaded[s], 16)

            def load_gb(l, j):
                wait_apart(xn_ready, count(xn_ready, l, 4 * j + 4))
                eng.dma_start(gb[:, :, :].rearrange("p a n -> p (a n)"),
                              ln_gb_v[bass.ds(3 * l + j, 1), :].broadcast_to([P, 2 * D])).then_inc(gb_loaded, 16)

            def ffn(l, w):
                b = BASE[2 * w]
                load_ffn_in(l, w, b, b, 0, 0)
                load_ffn_in(l, w, b + 1, b + 1, 1, 0)
                with eng.Fori(1, NCH) as c:
                    load_ffn_in(l, w, b + 2, b + 3 * c - 1, 0, c)
                    load_ffn_in(l, w, b + 3, b + 3 * c, 1, c)
                    load_ffn_out(l, w, b + 4, b + 3 * c + 1, c - 1)
                load_gb(l, 2 * w)
                load_ffn_out(l, w, b + FFN_UNITS - 1, b + FFN_UNITS - 1, NCH - 1)

            def load_unit(l, u, view, source):
                wait_slot(l, BASE[1] + u)
                k = source.shape[1] // 2
                for j in range(2):
                    eng.dma_start(view[:, j * k:j * k + k, :], source[:, j * k:j * k + k, :])\
                       .then_inc(raw_loaded[u % RING], 16)

            def mixer(l):
                w_l = w_in_v[bass.ds(l, 1)].rearrange("a p k n -> (a p) k n")
                o_l = w_o_v[bass.ds(l, 1)].rearrange("a p k n -> (a p) k n")
                for g, col in enumerate((COL_CONV, COL_CQ, COL_CK, COL_CV, COL_FQK)):
                    for half in range(2):
                        u = 2 * g + half
                        view = raw[:, u % RING, 0:UNIT].rearrange("p (k n) -> p k n", k=4)
                        load_unit(l, u, view, w_l[:, 4 * half:4 * half + 4, col:col + BANK])
                    if g == 0:
                        eng.dma_start(small[:, :], rows[bass.ds(l, 1), 0, :].broadcast_to([P, rows.shape[2]]))\
                           .then_inc(small_loaded, 16)
                        eng.dma_start(cwb[:, :, :].rearrange("p c k -> p (c k)"),
                                      conv_wb[bass.ds(l, 1)].rearrange("a p n -> (a p) n")).then_inc(small_loaded, 16)
                load_gb(l, 1)
                view = raw[:, 10 % RING, :].rearrange("p (k n) -> p k n", k=KT)
                load_unit(l, 10, view, w_l[:, :, COL_FV:COL_FV + FVF])
                for u, (k0, _) in WO_KT.items():
                    view = raw[:, u % RING, 0:UNIT].rearrange("p (k n) -> p k n", k=2)
                    load_unit(l, u, view, o_l[:, k0:k0 + 2, :])

            eng.dma_start(xn[:, 0, :], x[0:P, :]).then_inc(x0_loaded, 16)
            eng.dma_start(cst[:, 0:EARLY], consts[:, 0:EARLY]).then_inc(cst_loaded, 16)
            with eng.Fori(0, DEPTH) as l:
                ffn(l, 0)
                mixer(l)
                ffn(l, 1)
            for t in range(T):
                eng.wait_ge(xn_ready, count(xn_ready, DEPTH, HALVES * (t + 1)))
                eng.dma_start(out[t * P:(t + 1) * P, :], xn[:, t, :]).then_inc(stored, 16)
            eng.wait_ge(stored, 16 * T)

        @block.tensor
        def _(eng):
            def wait_unit(l, u):
                eng.wait_ge(lo_done, unit_count(l, u) + RING)

            def frees(first, signal):
                if signal is not None:
                    first.then_inc(signal, 1)

            def transposes(dst, blocks, last_unit=None):
                for n, blk in enumerate(blocks):
                    m = eng.transpose(dst[:, n * P:(n + 1) * P], blk, ident)
                    if n == 0:
                        frees(m, last_unit)
                return m

            def stage_x(l, j, t):
                for h in range(HALVES):
                    if t > 0:
                        eng.wait_ge(xT_ready, count(xT_ready, l, 4 * j + h + 1))
                    eng.wait_ge(xn_ready, count(xn_ready, l, 4 * j + 2 * t + h + 1))
                    blocks = [xn[:, t, (4 * h + k) * P:(4 * h + k + 1) * P] for k in range(4)]
                    transposes(bank[2 + h], blocks, unit_used if t == h == 0 else None).then_inc(xT_psum, 1)

            def open_sums(t):
                for h in range(HALVES):
                    m = eng.matmul(ybank[2 * t + h][:, :], xT_hi[:, 0, 0:P], xT_hi[:, 0:4, 0:P],
                                   start=True, stop=False).then_inc(sum_open, 1)
                return m

            def project(dst, slot, half, t, width=BANK, kts=4, last_unit=None, parts=("hi", "lo"),
                        ks=None):
                wh = w_hi[:, slot, 0:kts * width].rearrange("p (k n) -> p k n", k=kts)
                wl = w_lo[:, slot, 0:kts * width].rearrange("p (k n) -> p k n", k=kts)
                tok = slice(t * P, (t + 1) * P)
                for k in ks or range(kts):
                    kk = kts * half + k
                    if "hi" in parts:
                        m = eng.matmul(dst, xT_hi[:, kk, tok], wh[:, k, :], start=kk == 0, stop=False)
                        if k == 0:
                            frees(m, last_unit)
                        m = eng.matmul(dst, xT_hi[:, kk, tok], wl[:, k, :], start=False, stop=False)
                    if "lo" in parts:
                        m = eng.matmul(dst, xT_lo[:, kk, tok], wh[:, k, :], start=False, stop=kk == KT - 1)
                return m

            def first_unit(l, j, t, dst):
                n = 4 * j + 2 * t + 1
                eng.wait_ge(xT_hi_done, count(xT_hi_done, l, n))
                project(dst, 0, 0, t, parts=("hi",))
                eng.wait_ge(xT_ready, count(xT_ready, l, n))
                return project(dst, 0, 0, t, parts=("lo",))

            def out_product(slot, aT, t, ends=None, last_unit=None, halves=range(HALVES)):
                aT_hi, aT_lo = aT
                wh = w_hi[:, slot, 0:UNIT].rearrange("p (k n) -> p k n", k=2)
                wl = w_lo[:, slot, 0:UNIT].rearrange("p (k n) -> p k n", k=2)
                tok = slice(t * P, (t + 1) * P)
                for h in halves:
                    dst, cols = ybank[2 * t + h][:, :], slice(h * BANK, (h + 1) * BANK)
                    for k in range(2):
                        m = eng.matmul(dst, aT_hi[:, k, tok], wh[:, k, cols], start=False, stop=False)
                        if h == k == 0:
                            frees(m, last_unit)
                        eng.matmul(dst, aT_hi[:, k, tok], wl[:, k, cols], start=False, stop=False)
                        m = eng.matmul(dst, aT_lo[:, k, tok], wh[:, k, cols], start=False,
                                       stop=ends is not None and k == 1)
                    if ends is not None:
                        m.then_inc(ends, 1)
                return m

            def hidden_T(l, f, c):
                eng.wait_ge(h_ready, count(h_ready, l, (f + 1) * T + c * T))
                transposes(bank[0], [hid[:, t, j * P:(j + 1) * P] for j in range(2) for t in range(T)])\
                    .then_inc(hT_psum, 1)

            def ffn(l, w):
                b, f = BASE[2 * w], w * NCH
                s = [(b + n) % RING for n in range(RING)]
                for t in range(T):
                    stage_x(l, 2 * w, t)
                    if t == 0:
                        wait_unit(l, b)
                    else:
                        open_sums(0)
                        open_sums(1)
                    m = first_unit(l, 2 * w, t, bank[t][:, :])
                    if t == 0:
                        wait_unit(l, b + 1)
                    else:
                        m.then_inc(unit_used, 1)
                    eng.wait_ge(xT_ready, count(xT_ready, l, 8 * w + 2 * t + 2))
                    project(bank[t][:, :], s[1], 1, t).then_inc(gu_done, 1)

                def gate_up(c, last_unit=None):
                    if last_unit is None:
                        eng.wait_ge(h_ready, count(h_ready, l, f * T + c * T))
                    wait_unit(l, b + 3 * c - 1)
                    project(bank[2][:, :], s[2], 0, 0, last_unit=last_unit)
                    project(bank[3][:, :], s[2], 0, 1).then_inc(unit_used, 1)
                    hidden_T(l, f, c - 1)
                    wait_unit(l, b + 3 * c)
                    for t in range(T):
                        project(bank[2 + t][:, :], s[0], 1, t).then_inc(gu_done, 1)
                    wait_unit(l, b + 3 * c + 1)
                    eng.wait_ge(hT_ready, count(hT_ready, l, f + c))

                def chunk(c, last_unit=None):
                    gate_up(c, last_unit)
                    if last_unit is not None:
                        eng.wait_ge(sum_begun, count(sum_begun, l, 8 * w + T * HALVES))
                    out_product(s[1], hT[0], 0, last_unit=unit_used)
                    out_product(s[1], hT[0], 1).then_inc(unit_used, 1)

                chunk(1, unit_used)
                with eng.Fori(2, NCH - 1) as c:
                    chunk(c)
                gate_up(NCH - 1)
                out_product(s[1], hT[0], 0, last_unit=unit_used)
                hidden_T(l, f, NCH - 1)
                out_product(s[1], hT[0], 1, halves=(0,))
                wait_unit(l, b + FFN_UNITS - 1)
                eng.wait_ge(hT_ready, count(hT_ready, l, f + NCH))
                out_product(s[2], hT[1], 0, ends=y_done)
                out_product(s[1], hT[0], 1, halves=(1,)).then_inc(unit_used, 1)
                out_product(s[2], hT[1], 1, ends=y_done)

            def score_slot(l, s):
                kind, h = SLOTS[s]
                b = bank[s % 2]
                if s < 2:
                    eng.wait_ge(cv_ready, count(cv_ready, l, s + 1))
                else:
                    before, hb = SLOTS[s - 2]
                    if before == "head":
                        eng.wait_ge(exp_done, count(exp_done, l, hb + 1))
                    elif before in ("fq", "fk"):
                        eng.wait_ge(qkT_ready, count(qkT_ready, l, 5 + (before == "fk")))
                    elif before == "conv":
                        eng.wait_ge(cln_ready, count(cln_ready, l, T))
                    else:
                        eng.wait_ge(yaT_ready, count(yaT_ready, l, 1))
                if kind in ("fq", "fk"):
                    eng.wait_ge(fqk_ready, count(fqk_ready, l, T))
                    o = FOX_H * HD * (kind == "fk")
                    transposes(b, [fqk[:, t, o + p * P:o + (p + 1) * P] for p in range(2) for t in range(T)])\
                        .then_inc(qk_psum, 1)
                elif kind == "conv":
                    eng.wait_ge(conv_step, count(conv_step, l, CB * CONV_K))
                    transposes(b, [acc[:, cb, t * P:(t + 1) * P] for t in range(T) for cb in range(CB)])\
                        .then_inc(convT_psum, 1)
                elif kind == "convy":
                    eng.wait_ge(ya_ready, count(ya_ready, l, 1))
                    transposes(b, [yb[:, t, cb * P:(cb + 1) * P] for cb in range(CB) for t in range(T)])\
                        .then_inc(yaT_psum, 1)
                else:
                    fox = h >= DIL_H
                    n = h - DIL_H * fox
                    qs, ks = (fqT, fkT) if fox else (qT, kT)
                    r = slice((n % 2) * HD, (n % 2 + 1) * HD)
                    eng.wait_ge(qkT_ready, count(qkT_ready, l, 2 * T + 2 * fox))
                    m = eng.matmul(b[:, 0:CAUSAL], ident_r[:, :], mask_hi[:, int(fox), :], start=True, stop=False)
                    frees(m, unit_used if s in FREES_AT else None)
                    if fox:
                        eng.wait_ge(lg_ready, count(lg_ready, l, 1))
                        eng.matmul(b[:, 0:P], tri_le, lg[:, n, 0:P], start=False, stop=False)
                        eng.matmul(b[:, P:2 * P], ones, lg[:, n, 0:P], start=False, stop=False)
                        eng.matmul(b[:, P:CAUSAL], tri_le, lg[:, n, P:CAUSAL], start=False, stop=False)
                    else:
                        eng.matmul(b[:, 0:CAUSAL], ident_r[:, :], mask_lo[:, :], start=False, stop=False)
                    eng.matmul(b[:, 0:P], qs[r, n // 2, 0:P], ks[r, n // 2, 0:P], start=False, stop=False)
                    eng.matmul(b[:, P:CAUSAL], qs[r, n // 2, P:SEQ], ks[r, n // 2, :], start=False, stop=True)\
                       .then_inc(s_done, 1)

            def probs_T(l, h):
                eng.wait_ge(p_ready, count(p_ready, l, h + 1))
                if h > 0:
                    eng.wait_ge(pT_ready, count(pT_ready, l, h))
                transposes(bank[2], [prob[:, h % 2, i * P:(i + 1) * P] for i in range(3)]).then_inc(pT_psum, 1)

            def values(l, h):
                eng.wait_ge(pT_ready, count(pT_ready, l, h + 1))
                if h >= 2 and h % 2 == 0:
                    eng.wait_ge(y_ready, count(y_ready, l, h // 2))
                if h >= DIL_H:
                    eng.wait_ge(fv_ready, count(fv_ready, l, T))
                    v, n = fv, h - DIL_H
                else:
                    v, n = cv, h
                r = slice((h % 2) * HD, (h % 2 + 1) * HD)
                eng.matmul(bank[3][r, 0:SEQ], v[:, 0, n * HD:(n + 1) * HD], probT[:, h % 2, 0:SEQ],
                           start=True, stop=False)
                eng.matmul(bank[3][r, P:SEQ], v[:, 1, n * HD:(n + 1) * HD], probT[:, h % 2, SEQ:CAUSAL],
                           start=False, stop=True).then_inc(pv_done, 1)

            def fill(l, u, t, half):
                if u == "open":
                    if t == 0:
                        eng.wait_ge(fqk_ready, count(fqk_ready, l, T))
                    else:
                        eng.wait_ge(fz_ready, count(fz_ready, l, T))
                    open_sums(t)
                    return
                s = u % RING
                if t == half == 0:
                    wait_unit(l, BASE[1] + u)
                if u in (8, 9):
                    if u == 8 and t == half == 0:
                        eng.wait_ge(rope_mul, count(rope_mul, l, T))
                    m = project(ybank[t][:, :], s, u - 8, t, ks=range(2 * half, 2 * half + 2))
                    if u == 9 and half == 1:
                        m.then_inc(proj_done, 1)
                    elif t == half == 1:
                        m.then_inc(unit_used, 1)
                elif u == 10:
                    if t == half == 0:
                        eng.wait_ge(rope_mul, count(rope_mul, l, 2 * T))
                    m = project(ybank[2 + t][:, 0:FVF], s, 0, t, FVF, KT, unit_used if t == half == 0 else None,
                                ks=range(4 * half, 4 * half + 4))
                    if half == 1:
                        m.then_inc(proj_done, 1)
                else:
                    if t == half == 0:
                        if u == 13:
                            eng.wait_ge(yaT_ready, count(yaT_ready, l, 1))
                        else:
                            eng.wait_ge(y_ready, count(y_ready, l, {11: 2, 12: 4, 14: 6}[u]))
                    if u == 11 and half == 0:
                        eng.wait_ge(sum_begun, count(sum_begun, l, 4 + 2 * t + 2))
                    k0 = WO_KT[u][0]
                    yT = yT_hi[:, k0:k0 + 2, :], yT_lo[:, k0:k0 + 2, :]
                    m = out_product(s, yT, t, ends=y_done if u == 14 else None, halves=(half,))
                    if u < 14 and t == half == 1:
                        m.then_inc(unit_used, 1)

            def rotated_T(l, which, last_unit):
                for n in which:
                    eng.wait_ge(rope_ready, count(rope_ready, l, n + 1))
                    if n == 1:
                        eng.wait_ge(uT_ready, count(uT_ready, l, 1))
                    if n >= 2:
                        eng.wait_ge(qkT_ready, count(qkT_ready, l, n - 1))
                    transposes(bank[3 - n % T], [qk[:, n % T, p * P:(p + 1) * P] for p in range(4)],
                               last_unit if n % T == 0 else None).then_inc(qk_psum, 1)

            def mixer(l):
                b = BASE[1]
                for t in range(T):
                    stage_x(l, 1, t)
                    if t == 0:
                        wait_unit(l, b)
                    m = first_unit(l, 1, t, bank[t][:, :])
                    if t == T - 1:
                        m.then_inc(unit_used, 1)
                    else:
                        wait_unit(l, b + 1)
                    eng.wait_ge(xT_ready, count(xT_ready, l, 4 + 2 * t + 2))
                    project(bank[t][:, :], 1, 1, t).then_inc(proj_done, 1)
                for g, dst in enumerate((ybank[0:2], ybank[2:4], bank[0:2]), 1):
                    if g == 3:
                        eng.wait_ge(u_ready, count(u_ready, l, T))
                    for half in range(2):
                        u = 2 * g + half
                        wait_unit(l, b + u)
                        for t in range(T):
                            m = project(dst[t][:, :], u % RING, half, t,
                                        last_unit=unit_used if g == 1 and half == t == 0 else None)
                            if half == 1:
                                m.then_inc(proj_done, 1)
                        if half == 0:
                            m.then_inc(unit_used, 1)
                        if g == 3 and half == 0:
                            rotated_T(l, range(2, 4), None)
                    if g == 1:
                        eng.wait_ge(u_ready, count(u_ready, l, T))
                        transposes(bank[2], [conv_u[:, t, cb * P:(cb + 1) * P] for cb in range(CB) for t in range(T)],
                                   unit_used).then_inc(uT_psum, 1)
                    elif g == 2:
                        rotated_T(l, range(2), unit_used)
                eng.wait_ge(setup_done, 3)
                for s in range(STEPS):
                    if s < len(SLOTS):
                        score_slot(l, s)
                    if 0 <= s - 1 < len(SLOTS) and SLOTS[s - 1][0] == "head":
                        probs_T(l, SLOTS[s - 1][1])
                    if 0 <= s - 2 and SLOTS[s - 2][0] == "head":
                        values(l, SLOTS[s - 2][1])
                    for part in FILL[s]:
                        fill(l, *part)
                for part in TAIL:
                    fill(l, *part)

            eng.sem_inc(unit_used, RING - 1)
            eng.wait_ge(cst_loaded, 16)
            with eng.Fori(0, DEPTH) as l:
                ffn(l, 0)
                mixer(l)
                ffn(l, 1)

        @block.scalar
        def _(eng):
            def split_hi(l, b, u, c=0):
                s = (b + u) % RING
                width = SLOT if b == BASE[1] and u == 10 and isinstance(c, int) else UNIT
                eng.wait_ge(raw_loaded[s], slot_load(l, b + u, c))
                eng.wait_ge(unit_used, unit_count(l, b + u + 3 * c))
                eng.activation(w_hi[:, s, 0:width], raw[:, s, 0:width], ACT.Copy).then_inc(hi_done, 1)

            def stage_hi(l, j, tiles):
                for t in tiles:
                    for h in range(HALVES):
                        eng.wait_ge(xT_psum, count(xT_psum, l, 4 * j + 2 * t + h + 1))
                        eng.activation(xT_hi[:, 4 * h:4 * h + 4, t * P:(t + 1) * P],
                                       bank[2 + h][:, :].rearrange("p (k n) -> p k n", k=4), ACT.Copy)\
                           .then_inc(xT_hi_done, 1)

            def begin_sum(l, j, t):
                for h in range(HALVES):
                    eng.wait_ge(sum_open, count(sum_open, l, 4 * j + 2 * t + h + 1))
                    eng.activation(ybank[2 * t + h][:, :], xn[:, t, h * BANK:(h + 1) * BANK], ACT.Copy,
                                   scale=ALPHA / SCALE[j]).then_inc(sum_begun, 1)

            def silu(l, f, c, t, b0=2):
                eng.wait_ge(gu_done, count(gu_done, l, f * T + t + 1 + c * T))
                eng.activation(gate[:, t, :], bank[b0 + t][:, 0:CHUNK], ACT.Silu).then_inc(gate_ready, 1)

            def hidden_hi(l, f, c, buf=0):
                eng.wait_ge(hT_psum, count(hT_psum, l, f + 1 + c))
                eng.activation(hT[buf][0], bank[0][:, :].rearrange("p (k n) -> p k n", k=2), ACT.Copy)\
                   .then_inc(hT_hi_done, 1)

            def ffn(l, w):
                b, f = BASE[2 * w], w * NCH
                if w == 0:
                    split_hi(l, b, 0)
                stage_hi(l, 2 * w, (0,))
                if w == 0:
                    split_hi(l, b, 1)
                split_hi(l, b, 2)
                stage_hi(l, 2 * w, (1,))
                silu(l, f, 0, 0, 0)
                split_hi(l, b, 3)
                silu(l, f, 0, 1, 0)
                split_hi(l, b, 4)
                for t in range(T):
                    begin_sum(l, 2 * w, t)

                def chunk(c):
                    hidden_hi(l, f, c - 1)
                    split_hi(l, b, 2, c)
                    silu(l, f, c, 0)
                    silu(l, f, c, 1)

                with eng.Fori(1, NCH - 1) as c:
                    chunk(c)
                    split_hi(l, b, 3, c)
                    split_hi(l, b, 4, c)
                chunk(NCH - 1)
                if w == 0:
                    split_hi(l, b, 3, NCH - 1)
                hidden_hi(l, f, NCH - 1, 1)
                if w == 0:
                    split_hi(l, b, 4, NCH - 1)

            def mixer(l):
                b = BASE[1]
                stage_hi(l, 1, (0,))
                split_hi(l, b, 2)
                stage_hi(l, 1, (1,))
                for t in range(T):
                    eng.wait_ge(proj_done, count(proj_done, l, t + 1))
                    eng.activation(egate[:, t, :], bank[t][:, CONV_CH:2 * CONV_CH], ACT.Sigmoid)\
                       .then_inc(egate_ready, 1)
                    split_hi(l, b, 3 + t)
                split_hi(l, b, 5)
                eng.wait_ge(uT_psum, count(uT_psum, l, 1))
                eng.activation(uT[:, :, CONV_K - 1:], bank[2][:, :].rearrange("p (c n) -> p c n", c=CB), ACT.Copy)\
                   .then_inc(uT_ready, 1)
                split_hi(l, b, 6)
                split_hi(l, b, 7)
                for n in range(2 * T):
                    t = n % T
                    if n == T:
                        split_hi(l, b, 8)
                    eng.wait_ge(qk_psum, count(qk_psum, l, n + 1))
                    dst = (qT, kT)[n // T]
                    eng.activation(dst[:, :, t * P:(t + 1) * P], bank[3 - t][:, :].rearrange("p (k n) -> p k n", k=4),
                                   ACT.Copy, scale=HD ** -0.5 if n < T else 1.0).then_inc(qkT_ready, 1)
                split_hi(l, b, 9)
                for t in range(T):
                    eng.wait_ge(proj_done, count(proj_done, l, 3 * T + t + 1))
                    eng.activation(cv[:, t, :], bank[t][:, :], ACT.Copy).then_inc(cv_ready, 1)
                for s in range(STEPS):
                    if 0 <= s - 1 < len(SLOTS) and SLOTS[s - 1][0] == "head":
                        h = SLOTS[s - 1][1]
                        eng.wait_ge(pT_psum, count(pT_psum, l, h + 1))
                        eng.activation(probT[:, h % 2, :], bank[2][:, 0:CAUSAL], ACT.Copy).then_inc(pT_ready, 1)
                    kind, h = SLOTS[s] if s < len(SLOTS) else ("none", 0)
                    sc = bank[s % 2]
                    if kind == "head":
                        eng.wait_ge(mx_ready, count(mx_ready, l, h + 1))
                        for t, cols in enumerate((slice(0, P), slice(P, CAUSAL))):
                            e = eng.activation(prob[:, h % 2, cols], sc[:, cols], ACT.Exp,
                                               bias=negmax[:, h % 2, t:t + 1], accum_out=den[:, h % 2, t:t + 1])
                        e.then_inc(exp_done, 1)
                    elif kind in ("fq", "fk"):
                        n = 4 + (kind == "fk")
                        eng.wait_ge(qk_psum, count(qk_psum, l, n + 1))
                        dst = fqT if kind == "fq" else fkT
                        eng.activation(dst[:, :, :], sc[:, :].rearrange("p (k n) -> p k n", k=2), ACT.Copy,
                                       scale=HD ** -0.5 if kind == "fq" else 1.0).then_inc(qkT_ready, 1)
                    elif kind == "convy":
                        eng.wait_ge(yaT_psum, count(yaT_psum, l, 1))
                        eng.activation(yT_hi[:, 0:CB, :], sc[:, :].rearrange("p (k n) -> p k n", k=CB), ACT.Copy)\
                           .then_inc(yaT_hi_done, 1)
                    if s in FQK_AT:
                        t = FQK_AT[s]
                        eng.wait_ge(proj_done, count(proj_done, l, 4 * T + t + 1))
                        eng.activation(fqk[:, t, :], ybank[t][:, :], ACT.Copy).then_inc(fqk_ready, 1)
                    if s in FV_AT:
                        t = FV_AT[s]
                        eng.wait_ge(proj_done, count(proj_done, l, 5 * T + t + 1))
                        eng.activation(fv[:, t, :], ybank[2 + t][:, 0:FOX_H * HD], ACT.Copy).then_inc(fv_ready, 1)
                    if s == LF_STEP:
                        eng.wait_ge(fe_ready, count(fe_ready, l, 1))
                        eng.activation(fl[:, :, :], fe[:, :, :], ACT.Exp).then_inc(fl_ready, 1)
                        eng.wait_ge(fl_ready, count(fl_ready, l, 1))
                        eng.activation(fl[:, :, :], fl[:, :, :], ACT.Ln, bias=1.0).then_inc(fl_ready, 1)
                    if s == CONV_SLOT + 1:
                        eng.wait_ge(cln_ready, count(cln_ready, l, T))
                        eng.activation(yb[:, :, :], ya[:, :, :], ACT.Silu).then_inc(ya_ready, 1)
                    if s in BEGIN_AT:
                        begin_sum(l, 1, BEGIN_AT[s])
                    if s in HI_AT:
                        split_hi(l, b, HI_AT[s])
                    if s >= 2 and SLOTS[s - 2][0] == "head" and SLOTS[s - 2][1] % 2:
                        pair = SLOTS[s - 2][1] // 2
                        eng.wait_ge(pv_done, count(pv_done, l, 2 * pair + 2))
                        eng.activation(yT_hi[:, Y_KT[pair], :], bank[3][:, 0:SEQ], ACT.Copy).then_inc(y_hi_done, 1)
                split_hi(l, b, 16)

            eng.wait_ge(pool_setup, 1)
            eng.activation(warm[:, :], minus_half[:, :], ACT.Silu)
            with eng.Fori(0, DEPTH) as l:
                ffn(l, 0)
                mixer(l)
                ffn(l, 1)

        @block.vector
        def _(eng):
            def split_lo(l, b, u, c=0):
                s = (b + u) % RING
                width = SLOT if b == BASE[1] and u == 10 and isinstance(c, int) else UNIT
                eng.wait_ge(hi_done, count(hi_done, l, b + u + 1 + 3 * c))
                eng.tensor_tensor(w_lo[:, s, 0:width], raw[:, s, 0:width], w_hi[:, s, 0:width].bitcast(F32),
                                  ALU.subtract).then_inc(lo_done, 1)

            def stage_lo(l, j, t):
                for h in range(HALVES):
                    eng.wait_ge(xT_hi_done, count(xT_hi_done, l, 4 * j + 2 * t + h + 1))
                    part = (slice(None), slice(4 * h, 4 * h + 4), slice(t * P, (t + 1) * P))
                    eng.tensor_tensor(xT_lo[part], bank[2 + h][:, :].rearrange("p (k n) -> p k n", k=4),
                                      xT_hi[part].bitcast(F32), ALU.subtract).then_inc(xT_ready, 1)

            def wait_apart(semaphore, value, n):
                eng.wait_ge(semaphore, value)
                eng.memset(carrier[:, n:n + 1], 0.0)

            def layer_norm(l, j, next_unit):
                def step(t, k):
                    return count(ln_step, l, 5 * (T * j + t) + k)

                for t in range(T):
                    for h in range(HALVES):
                        eng.wait_ge(y_done, count(y_done, l, HALVES * (T * j + t) + h + 1))
                        eng.bn_stats(stats[:, t, h, :], ybank[2 * t + h][:, :]).then_inc(ln_step, 1)
                    wait_apart(ln_step, step(t, 2), t)
                    eng.bn_aggr(mv[:, t, :], stats[:, t, :, :].rearrange("p a b -> p (a b)")).then_inc(ln_step, 1)
                    eng.wait_ge(ln_step, step(t, 3))
                    eng.tensor_scalar(vareps[:, t:t + 1], mv[:, t, 1:2], EPS / SCALE[j] ** 2, None, ALU.add)\
                       .then_inc(var_ready, 1)
                    if t == 0:
                        eng.wait_ge(gb_loaded, count(gb_loaded, l, 16 * (j + 1)))
                    for h in range(HALVES):
                        cols = slice(h * BANK, (h + 1) * BANK)
                        eng.scalar_tensor_tensor(xn[:, t, cols], ybank[2 * t + h][:, :], mv[:, t, 0:1], gb[:, 0, cols],
                                                 ALU.subtract, ALU.mult).then_inc(ln_step, 1)
                    eng.wait_ge(rstd_ready, count(rstd_ready, l, RSTD_AT[j] + t + 1))
                    for h in range(HALVES):
                        cols = slice(h * BANK, (h + 1) * BANK)
                        eng.wait_ge(ln_step, step(t, 4 + h))
                        eng.scalar_tensor_tensor(xn[:, t, cols], xn[:, t, cols], rstd[:, t:t + 1], gb[:, 1, cols],
                                                 ALU.mult, ALU.add).then_inc(xn_ready, 1)
                    if j < 2:
                        if t == 0:
                            split_lo(l, 0, next_unit)
                        stage_lo(l, j + 1, t)

            def gated(l, f, c, t, b0=2):
                eng.wait_ge(gate_ready, count(gate_ready, l, f * T + t + 1 + c * T))
                eng.tensor_tensor(hid[:, t, :], gate[:, t, :], bank[b0 + t][:, CHUNK:2 * CHUNK], ALU.mult)\
                   .then_inc(h_ready, 1)

            def hidden_lo(l, f, c, buf=0):
                hi, lo = hT[buf]
                eng.wait_ge(hT_hi_done, count(hT_hi_done, l, f + 1 + c))
                eng.tensor_tensor(lo, bank[0][:, :].rearrange("p (k n) -> p k n", k=2), hi.bitcast(F32),
                                  ALU.subtract).then_inc(hT_ready, 1)

            def ffn(l, w):
                b, f = BASE[2 * w], w * NCH
                if w == 0:
                    split_lo(l, b, 0)
                    stage_lo(l, 0, 0)
                    split_lo(l, b, 1)
                    stage_lo(l, 0, 1)
                split_lo(l, b, 2)
                gated(l, f, 0, 0, 0)
                split_lo(l, b, 3)
                gated(l, f, 0, 1, 0)
                split_lo(l, b, 4)

                def chunk(c):
                    hidden_lo(l, f, c - 1)
                    split_lo(l, b, 2, c)
                    gated(l, f, c, 0)
                    gated(l, f, c, 1)

                with eng.Fori(1, NCH - 1) as c:
                    chunk(c)
                    split_lo(l, b, 3, c)
                    split_lo(l, b, 4, c)
                chunk(NCH - 1)
                hidden_lo(l, f, NCH - 1, 1)
                if w == 0:
                    split_lo(l, b, 3, NCH - 1)
                layer_norm(l, 2 * w, BASE[1] + 1)

            def gated_conv_input(l, t):
                eng.wait_ge(egate_ready, count(egate_ready, l, t + 1))
                eng.tensor_tensor(conv_u[:, t, :], bank[t][:, 0:CONV_CH], egate[:, t, :], ALU.mult)\
                   .then_inc(u_ready, 1)

            def rope(l, n):
                t, src = n % T, ybank[n]
                eng.wait_ge(proj_done, count(proj_done, l, T + n + 1))
                if n > 0:
                    eng.wait_ge(rope_ready, count(rope_ready, l, n))
                eng.tensor_tensor(rope_c[:, :].rearrange("p (g e) -> p g e", e=32),
                                  src[:, :].rearrange("p (g e) -> p g e", e=32),
                                  cos_t[:, t:t + 1, :].broadcast_to([P, 2 * DIL_H, 32]), ALU.mult)
                halves = dict(h=DIL_H, s=2)
                swapped = src[:, :].rearrange("p (h s e) -> p h s e", **halves)[:, :, ::-1, :]
                sin4 = sin_t[:, t, :].rearrange("p (h s e) -> p h s e", h=1, s=2).broadcast_to([P, DIL_H, 2, 32])
                eng.tensor_tensor(rope_s[:, :].rearrange("p (h s e) -> p h s e", **halves), swapped, sin4, ALU.mult)\
                   .then_inc(rope_mul, 1)

            def taps(l, which):
                for k in which:
                    for cb in range(CB):
                        src, w = uT[:, cb, k:k + SEQ], cwb[:, cb, k:k + 1]
                        if k == 0:
                            eng.tensor_scalar(acc[:, cb, :], src, w, cwb[:, cb, CONV_K:CONV_K + 1], ALU.mult, ALU.add)\
                               .then_inc(conv_step, 1)
                        else:
                            eng.wait_ge(conv_step, count(conv_step, l, CB * (k - 1) + cb + 1))
                            eng.scalar_tensor_tensor(acc[:, cb, :], src, w, acc[:, cb, :], ALU.mult, ALU.add)\
                               .then_inc(conv_step, 1)

            def conv_norm_first(l):
                src = bank[CONV_SLOT % 2]
                eng.wait_ge(convT_psum, count(convT_psum, l, 1))
                for t in range(T):
                    eng.bn_stats(stats[:, t, 0, :], src[:, t * CONV_CH:(t + 1) * CONV_CH]).then_inc(cln_step, 1)
                for t in range(T):
                    wait_apart(cln_step, count(cln_step, l, t + 1), T + t)
                    eng.bn_aggr(mv[:, t, :], stats[:, t, 0, :]).then_inc(cln_step, 1)
                for t in range(T):
                    eng.wait_ge(cln_step, count(cln_step, l, T + t + 1))
                    eng.tensor_scalar(vareps[:, t:t + 1], mv[:, t, 1:2], EPS, None, ALU.add).then_inc(var_ready, 1)
                    eng.scalar_tensor_tensor(ya[:, t, :], src[:, t * CONV_CH:(t + 1) * CONV_CH], mv[:, t, 0:1], conv_g,
                                             ALU.subtract, ALU.mult).then_inc(cln_step, 1)
                for t in range(T):
                    eng.wait_ge(rstd_ready, count(rstd_ready, l, RSTD_CONV + t + 1))
                    eng.wait_ge(cln_step, count(cln_step, l, 2 * T + t + 1))
                    eng.scalar_tensor_tensor(ya[:, t, :], ya[:, t, :], rstd[:, t:t + 1], conv_b, ALU.mult, ALU.add)\
                       .then_inc(cln_ready, 1)

            def log_gates(l):
                eng.wait_ge(fl_ready, count(fl_ready, l, 2))
                eng.scalar_tensor_tensor(lf[:, :, :], fz[:, :, :], 0.0, fl[:, :, :], ALU.min, ALU.subtract)\
                   .then_inc(lf_ready, 1)
                eng.wait_ge(lf_ready, count(lf_ready, l, 1))
                for h in range(FOX_H):
                    for t, cols in enumerate((slice(0, P), slice(P, CAUSAL))):
                        e = eng.tensor_scalar(lg[:, h, cols], tri_after[:, cols], lf[:, t, h:h + 1], None, ALU.mult)
                e.then_inc(lg_ready, 1)

            def row_max(l, s, h):
                eng.wait_ge(s_done, count(s_done, l, h + 1))
                for t, cols in enumerate((slice(0, P), slice(P, CAUSAL))):
                    e = eng.tensor_reduce(negmax[:, h % 2, t:t + 1], bank[s % 2][:, cols], AX.X, ALU.max, negate=True)
                e.then_inc(mx_ready, 1)

            def normalise(l, h):
                eng.wait_ge(exp_done, count(exp_done, l, h + 1))
                eng.reciprocal(rden[:, h % 2, :], den[:, h % 2, :]).then_inc(rden_done, 1)
                eng.wait_ge(rden_done, count(rden_done, l, h + 1))
                for t, cols in enumerate((slice(0, P), slice(P, CAUSAL))):
                    e = eng.tensor_scalar(prob[:, h % 2, cols], prob[:, h % 2, cols], rden[:, h % 2, t:t + 1], None,
                                          ALU.mult)
                e.then_inc(p_ready, 1)

            def y_split_lo(l, s):
                if s >= 2 and SLOTS[s - 2][0] == "head" and SLOTS[s - 2][1] % 2:
                    pair = SLOTS[s - 2][1] // 2
                    eng.wait_ge(y_hi_done, count(y_hi_done, l, pair + 1))
                    eng.tensor_tensor(yT_lo[:, Y_KT[pair], :], bank[3][:, 0:SEQ], yT_hi[:, Y_KT[pair], :].bitcast(F32),
                                      ALU.subtract).then_inc(y_ready, 1)

            def mixer(l):
                b = BASE[1]
                eng.wait_ge(setup_done, 3)
                split_lo(l, b, 2)
                for t in range(T):
                    gated_conv_input(l, t)
                    split_lo(l, b, 3 + t)
                split_lo(l, b, 5)
                rope(l, 0)
                rope(l, 1)
                split_lo(l, b, 6)
                eng.wait_ge(small_loaded, count(small_loaded, l, 32))
                eng.wait_ge(uT_ready, count(uT_ready, l, 1))
                taps(l, range(1))
                taps(l, TAPS_AT["unit", 5])
                split_lo(l, b, 7)
                rope(l, 2)
                taps(l, TAPS_AT["unit", 6][:2])
                rope(l, 3)
                taps(l, TAPS_AT["unit", 6][2:])
                split_lo(l, b, 8)
                taps(l, TAPS_AT["unit", 7])
                split_lo(l, b, 9)
                for s in range(STEPS):
                    kind, h = SLOTS[s] if s < len(SLOTS) else ("none", 0)
                    if kind == "head":
                        row_max(l, s, h)
                    y_split_lo(l, s - 1)
                    step_taps = TAPS_AT.get(("step", s), ())
                    taps(l, step_taps[:1])
                    if kind == "head":
                        normalise(l, h)
                    taps(l, step_taps[1:])
                    if s in FV_AT:
                        t = FV_AT[s]
                        eng.wait_ge(fv_ready, count(fv_ready, l, t + 1))
                        eng.tensor_tensor(fz[:, t, :], ybank[2 + t][:, FOX_H * HD:FVF], fbias, ALU.add)\
                           .then_inc(fz_ready, 1)
                    if s == LF_STEP - 1:
                        eng.wait_ge(fz_ready, count(fz_ready, l, T))
                        eng.scalar_tensor_tensor(fe[:, :, :], fz[:, :, :], -1.0, fz[:, :, :], ALU.mult, ALU.min)\
                           .then_inc(fe_ready, 1)
                    if s == LF_STEP + 1:
                        log_gates(l)
                    if s == CONV_SLOT:
                        conv_norm_first(l)
                    if kind == "convy":
                        eng.wait_ge(yaT_hi_done, count(yaT_hi_done, l, 1))
                        eng.tensor_tensor(yT_lo[:, 0:CB, :], bank[s % 2][:, :].rearrange("p (k n) -> p k n", k=CB),
                                          yT_hi[:, 0:CB, :].bitcast(F32), ALU.subtract).then_inc(yaT_ready, 1)
                    if s - 1 in HI_AT:
                        split_lo(l, b, HI_AT[s - 1])
                y_split_lo(l, STEPS - 1)
                layer_norm(l, 1, BASE[2] + 1)

            eng.sem_inc(lo_done, RING)
            eng.memset(uT[:, :, 0:CONV_K - 1], 0.0)
            with eng.Fori(0, DEPTH) as l:
                ffn(l, 0)
                mixer(l)
                ffn(l, 1)

        @block.gpsimd
        def _(eng):
            def deviations(l, base):
                for t in range(T):
                    eng.wait_ge(var_ready, count(var_ready, l, base + t + 1))
                    eng.tensor_tensor(rstd[:, t:t + 1], vareps[:, t:t + 1], minus_half[:, t:t + 1], ALU.pow)\
                       .then_inc(rstd_ready, 1)

            eng.memset(minus_half[:, :], -0.5).then_inc(pool_setup, 1)
            eng.wait_ge(pool_setup, 1)
            eng.wait_ge(x0_loaded, 16)
            eng.sem_inc(xn_ready, HALVES)
            eng.wait_ge(raw_loaded[0], 32)
            eng.dma_start(xn[:, 1, :], x[P:SEQ, :]).then_inc(x1_loaded, 16)
            eng.wait_ge(x1_loaded, 16)
            eng.sem_inc(xn_ready, HALVES)
            eng.wait_ge(raw_loaded[2], 32)
            eng.dma_start(cst[:, EARLY:], consts[:, EARLY:]).then_inc(tables_loaded, 16)
            eng.wait_ge(tables_loaded, 16)
            eng.tensor_copy(ident_r[:, :], ident).then_inc(setup_done, 1)
            eng.tensor_copy(mask_hi[:, :, :], masks.rearrange("p (m n) -> p m n", m=2)).then_inc(setup_done, 1)
            eng.wait_ge(setup_done, 2)
            eng.tensor_tensor(mask_lo[:, :], masks[:, 0:CAUSAL], mask_hi[:, 0, :].bitcast(F32), ALU.subtract)\
               .then_inc(setup_done, 1)
            with eng.Fori(0, DEPTH) as l:
                deviations(l, RSTD_AT[0])
                for n in range(2 * T):
                    eng.wait_ge(rope_mul, count(rope_mul, l, n + 1))
                    if n >= T:
                        eng.wait_ge(qk_psum, count(qk_psum, l, n - T + 1))
                    eng.tensor_tensor(qk[:, n % T, :], rope_c[:, :], rope_s[:, :], ALU.add).then_inc(rope_ready, 1)
                deviations(l, RSTD_CONV)
                deviations(l, RSTD_AT[1])
                deviations(l, RSTD_AT[2])


def kernel(**inputs):
    import concourse.bacc as _bacc
    from concourse.bass_utils import run_bass_kernel_spmd as _run

    a = {k: np.ascontiguousarray(v) for k, v in inputs.items()}
    arrays = {
        "x": a["x"].reshape(SEQ, D), "w_in": a["w_in"], "w_o": a["w_o"],
        "ffn_in": a["ffn_w_in"], "ffn_out": a["ffn_w_out"],
        "ln_gb": np.concatenate([a["ln_g"], a["ln_b"]], axis=2),
        "conv_wb": np.ascontiguousarray(
            np.concatenate([a["conv_w"], a["conv_b"][:, None, :]], axis=1)
            .reshape(DEPTH, CONV_K + 1, CB, P).transpose(0, 3, 2, 1).reshape(DEPTH, P, CB * (CONV_K + 1))),
        "rows": np.concatenate([a["conv_ln_g"], a["conv_ln_b"], a["forget_bias"]], axis=1)[:, None, :],
        "consts": consts_array(),
    }
    arrays = {f"in_{k}": np.ascontiguousarray(v) for k, v in arrays.items()}
    nc = _bacc.Bacc("TRN2", target_bir_lowering=False, num_devices=1)
    args = [nc.dram_tensor(k, v.shape, mybir.dt.from_np(v.dtype), kind="ExternalInput").ap() for k, v in arrays.items()]
    out = nc.dram_tensor("out_dram", (SEQ, D), F32, kind="ExternalOutput").ap()
    trunk(nc, *args, out)
    r = _run(nc, [arrays], core_ids=[0])
    return r.results[0]["out_dram"].reshape(1, SEQ, D)
```
